# Optimizing a Trainium2 kernel written in Bass

```python
import math
import jax, jax.numpy as jnp
from jax import lax
import numpy as np

D_MODEL = 2048
BATCH = 1
SEQ = 256
DEPTH = 1

GRID_W = 64
CTX_LEN = 256
RET_HEADS = 4
RET_DK = 256
RET_DV = 256
GLA_HEADS = 4
GLA_DK = 128
GLA_DV = 256
GLA_LOW_RANK = 16
GLA_GATE_NORM = 16.0
CHUNK = 64
D_FF = ((8 * D_MODEL // 3 + 255) // 256) * 256
ROPE_BASE = 10000.0
EPS = 1e-6

RET_QK = RET_HEADS * RET_DK
RET_VW = RET_HEADS * RET_DV
GLA_KW = GLA_HEADS * GLA_DK
GLA_VW = GLA_HEADS * GLA_DV
SPLIT_SIZES = (RET_QK, RET_VW, GLA_KW, GLA_VW, 2 * GLA_LOW_RANK,
               RET_QK, RET_VW, GLA_KW, GLA_VW, D_MODEL, D_MODEL)
N_CTX_COLS = RET_QK + RET_VW + GLA_KW + GLA_VW + 2 * GLA_LOW_RANK
D_IN = sum(SPLIT_SIZES)

kernel_name = 'hybrid_retention_gla_block'

def rms_norm(t, w):
    tf = t.astype(jnp.float32)
    return tf * lax.rsqrt(jnp.mean(tf * tf, axis=-1, keepdims=True) + EPS) * w

def split_cols(p, sizes):
    offsets = []
    acc = 0
    for s in sizes[:-1]:
        acc += s
        offsets.append(acc)
    return jnp.split(p, offsets, axis=-1)

def to_heads(t, n_heads):
    b, l, _ = t.shape
    return t.reshape(b, l, n_heads, -1).transpose(0, 2, 1, 3).astype(jnp.float32)

def merge_heads(t):
    b, h, l, d = t.shape
    return t.transpose(0, 2, 1, 3).reshape(b, l, h * d)

def axial_rope_tables(pos_r, pos_c, dk):
    n_f = dk // 4
    inv = ROPE_BASE ** (-jnp.arange(n_f, dtype=jnp.float32) / n_f)
    ang = jnp.concatenate([pos_r[:, None] * inv, pos_c[:, None] * inv], axis=-1)
    return jnp.cos(ang), jnp.sin(ang)

def apply_rope(t, cos, sin):
    half = t.shape[-1] // 2
    t1, t2 = t[..., :half], t[..., half:]
    return jnp.concatenate([t1 * cos - t2 * sin, t1 * sin + t2 * cos], axis=-1)

def head_layer_norm(o):
    mu = jnp.mean(o, axis=-1, keepdims=True)
    var = jnp.mean(jnp.square(o - mu), axis=-1, keepdims=True)
    return (o - mu) * lax.rsqrt(var + EPS)

def head_rms_norm(o):
    return o * lax.rsqrt(jnp.mean(o * o, axis=-1, keepdims=True) + EPS)

def ctx_final_state(k, v, log_a):
    b = jnp.cumsum(log_a, axis=2)
    w = jnp.exp(b[:, :, -1:, :] - b)
    return jnp.einsum('bhjd,bhjv->bhdv', k * w, v)

def chunk_recurrence(q, k, v, log_a, s0, exclusive):
    bsz, nh, length, _ = q.shape
    dv = v.shape[-1]
    n_chunks = length // CHUNK
    scalar = log_a.shape[-1] == 1
    mask = jnp.tril(jnp.ones((CHUNK, CHUNK), dtype=bool), k=-1 if exclusive else 0)

    def chunks(t):
        return jnp.moveaxis(t.reshape(bsz, nh, n_chunks, CHUNK, t.shape[-1]), 2, 0)

    def step(s, inp):
        qc, kc, vc, ac = inp
        b = jnp.cumsum(ac, axis=2)
        b_last = b[:, :, -1:, :]
        diff = b[:, :, :, None, :] - b[:, :, None, :, :]
        decay = jnp.exp(jnp.where(mask[:, :, None], diff, -jnp.inf))
        if scalar:
            scores = jnp.einsum('bhid,bhjd->bhij', qc, kc) * decay[..., 0]
        else:
            scores = jnp.einsum('bhid,bhjd,bhijd->bhij', qc, kc, decay)
        o = (jnp.einsum('bhij,bhjv->bhiv', scores, vc)
             + jnp.einsum('bhid,bhdv->bhiv', qc * jnp.exp(b), s))
        s_new = (jnp.exp(b_last[:, :, 0, :, None]) * s
                 + jnp.einsum('bhjd,bhjv->bhdv', kc * jnp.exp(b_last - b), vc))
        return s_new, o

    _, o = lax.scan(step, s0, (chunks(q), chunks(k), chunks(v), chunks(log_a)))
    return jnp.moveaxis(o, 0, 2).reshape(bsz, nh, length, dv)

def bidirectional_recurrence(q, k, v, la_f, la_b, kc, vc, lac_f, lac_b):
    flip = lambda t: jnp.flip(t, axis=2)
    s_f = ctx_final_state(kc, vc, lac_f)
    s_b = ctx_final_state(flip(kc), flip(vc), flip(lac_b))
    o_f = chunk_recurrence(q, k, v, la_f, s_f, False)
    o_b = flip(chunk_recurrence(flip(q), flip(k), flip(v), flip(la_b), s_b, True))
    return o_f + o_b

def hybrid_mixer(h, hc, w_in, ret_decay, gla_a_up, gla_a_bias, ret_gn, gla_gn,
                 w_up_ret, w_up_gla, w_out, cos, sin):
    f32 = jnp.float32
    bsz, length, _ = h.shape
    lc = hc.shape[1]
    p = h @ w_in
    pc = hc @ w_in[:, :N_CTX_COLS]
    rk, rv, gk, gv, ga, rq, rg, gq, gg, gate_a, gate_b = split_cols(p, SPLIT_SIZES)
    rkc, rvc, gkc, gvc, gac = split_cols(pc, SPLIT_SIZES[:5])

    log_gamma = -jnp.exp(ret_decay.astype(f32))

    def ret_la(n, d):
        return jnp.broadcast_to(log_gamma[d][None, :, None, None], (bsz, RET_HEADS, n, 1))

    q_r = apply_rope(to_heads(rq, RET_HEADS), cos, sin) * (RET_DK ** -0.5)
    k_r = apply_rope(to_heads(rk, RET_HEADS), cos, sin)
    o_r = bidirectional_recurrence(q_r, k_r, to_heads(rv, RET_HEADS), ret_la(length, 0), ret_la(length, 1),
                                   to_heads(rkc, RET_HEADS), to_heads(rvc, RET_HEADS),
                                   ret_la(lc, 0), ret_la(lc, 1))
    o_r = merge_heads(head_layer_norm(o_r)) * ret_gn * jax.nn.silu(rg.astype(f32))
    y_ret = o_r @ w_up_ret

    def gla_la(a_low, d):
        z = a_low[..., d * GLA_LOW_RANK:(d + 1) * GLA_LOW_RANK] @ gla_a_up[d] + gla_a_bias[d]
        return to_heads(jax.nn.log_sigmoid(z.astype(f32)) / GLA_GATE_NORM, GLA_HEADS)

    q_g = to_heads(gq, GLA_HEADS) * (GLA_DK ** -0.5)
    o_g = bidirectional_recurrence(q_g, to_heads(gk, GLA_HEADS), to_heads(gv, GLA_HEADS),
                                   gla_la(ga, 0), gla_la(ga, 1),
                                   to_heads(gkc, GLA_HEADS), to_heads(gvc, GLA_HEADS),
                                   gla_la(gac, 0), gla_la(gac, 1))
    o_g = merge_heads(head_rms_norm(o_g)) * gla_gn * jax.nn.silu(gg.astype(f32))
    y_gla = o_g @ w_up_gla

    merged = jax.nn.sigmoid(gate_a.astype(f32)) * y_ret + jax.nn.sigmoid(gate_b.astype(f32)) * y_gla
    return merged @ w_out

def setup_inputs(seed: int = 0) -> dict:
    key = jax.random.key(seed)
    ks = jax.random.split(key, 24)
    f32 = jnp.float32

    def nrm(k, shape, scale):
        return jax.random.normal(k, shape, f32) * scale

    ret_init = np.log(-np.log(1.0 - np.exp(np.linspace(np.log(1.0 / 32), np.log(1.0 / 512), RET_HEADS))))
    ret_decay = jnp.asarray(ret_init, f32)[None, None, :] + nrm(ks[10], (DEPTH, 2, RET_HEADS), 0.05)
    return {
        'x': nrm(ks[0], (BATCH, SEQ, D_MODEL), 1.0),
        'c': nrm(ks[1], (BATCH, D_MODEL), 1.0),
        'ctx': nrm(ks[2], (BATCH, CTX_LEN, D_MODEL), 1.0),
        'c_ctx': nrm(ks[3], (D_MODEL,), 1.0),
        'w_mod': nrm(ks[4], (DEPTH, D_MODEL, 6 * D_MODEL), 0.5 * D_MODEL ** -0.5),
        'b_mod': nrm(ks[5], (DEPTH, 6 * D_MODEL), 0.01),
        'norm_mix_pre': 1.0 + nrm(ks[6], (DEPTH, D_MODEL), 0.05),
        'norm_mix_post': 1.0 + nrm(ks[7], (DEPTH, D_MODEL), 0.05),
        'norm_ffn_pre': 1.0 + nrm(ks[8], (DEPTH, D_MODEL), 0.05),
        'norm_ffn_post': 1.0 + nrm(ks[9], (DEPTH, D_MODEL), 0.05),
        'w_in': nrm(ks[11], (DEPTH, D_MODEL, D_IN), D_MODEL ** -0.5),
        'ret_decay': ret_decay,
        'gla_a_up': nrm(ks[12], (DEPTH, 2, GLA_LOW_RANK, GLA_KW), GLA_LOW_RANK ** -0.5),
        'gla_a_bias': nrm(ks[13], (DEPTH, 2, GLA_KW), 0.01),
        'ret_gn': 1.0 + nrm(ks[14], (DEPTH, RET_VW), 0.05),
        'gla_gn': 1.0 + nrm(ks[15], (DEPTH, GLA_VW), 0.05),
        'w_up_ret': nrm(ks[16], (DEPTH, RET_VW, D_MODEL), RET_VW ** -0.5),
        'w_up_gla': nrm(ks[17], (DEPTH, GLA_VW, D_MODEL), GLA_VW ** -0.5),
        'w_out': nrm(ks[18], (DEPTH, D_MODEL, D_MODEL), D_MODEL ** -0.5),
        'ffn_w_gate': nrm(ks[19], (DEPTH, D_MODEL, D_FF), D_MODEL ** -0.5),
        'ffn_w_up': nrm(ks[20], (DEPTH, D_MODEL, D_FF), D_MODEL ** -0.5),
        'ffn_w_down': nrm(ks[21], (DEPTH, D_FF, D_MODEL), D_FF ** -0.5),
    }

def reference(x, c, ctx, c_ctx, w_mod, b_mod, norm_mix_pre, norm_mix_post, norm_ffn_pre, norm_ffn_post,
              w_in, ret_decay, gla_a_up, gla_a_bias, ret_gn, gla_gn, w_up_ret, w_up_gla, w_out,
              ffn_w_gate, ffn_w_up, ffn_w_down):
    f32 = jnp.float32
    out_dtype = x.dtype
    length = x.shape[1]
    rows = length // GRID_W
    pos_r = jnp.repeat(jnp.arange(rows, dtype=f32), GRID_W)
    pos_c = jnp.tile(jnp.arange(GRID_W, dtype=f32), rows)
    cos, sin = axial_rope_tables(pos_r, pos_c, RET_DK)

    h_state = x.astype(f32)
    for i in range(DEPTH):
        mod = jax.nn.silu(c.astype(f32)) @ w_mod[i] + b_mod[i]
        sh1, sc1, g1, sh2, sc2, g2 = jnp.split(mod, 6, axis=-1)
        mod_c = jax.nn.silu(c_ctx.astype(f32)) @ w_mod[i][:, :2 * D_MODEL] + b_mod[i][:2 * D_MODEL]
        shc, scc = jnp.split(mod_c, 2)

        h = rms_norm(h_state, norm_mix_pre[i]) * (1.0 + sc1[:, None]) + sh1[:, None]
        hc = rms_norm(ctx, norm_mix_pre[i]) * (1.0 + scc) + shc
        y = hybrid_mixer(h, hc, w_in[i], ret_decay[i], gla_a_up[i], gla_a_bias[i], ret_gn[i], gla_gn[i],
                         w_up_ret[i], w_up_gla[i], w_out[i], cos, sin)
        h_state = h_state + g1[:, None] * rms_norm(y, norm_mix_post[i])

        h = rms_norm(h_state, norm_ffn_pre[i]) * (1.0 + sc2[:, None]) + sh2[:, None]
        y = (jax.nn.silu(h @ ffn_w_gate[i]) * (h @ ffn_w_up[i])) @ ffn_w_down[i]
        h_state = h_state + g2[:, None] * rms_norm(y, norm_ffn_post[i])
    return h_state.astype(out_dtype)


_drawn_inputs = setup_inputs


def setup_inputs(seed=0):
    import zlib

    import numpy as np

    out = dict(_drawn_inputs(seed))
    spreads = {}
    factors = {'b_mod': 3.098,
     'norm_mix_post': 3.506,
     'norm_ffn_pre': 2.85,
     'norm_ffn_post': 3.806,
     'gla_a_bias': 8.0,
     'ret_gn': 5.467,
     'gla_gn': 5.275}
    for name, (base, spread) in spreads.items():
        noise = np.random.default_rng([zlib.crc32(name.encode()), seed]).standard_normal(out[name].shape)
        drawn = base * np.exp(spread * noise) if base else spread * noise
        out[name] = __import__('jax').numpy.asarray(drawn.astype(out[name].dtype))
    for name, factor in factors.items():
        out[name] = (out[name] * factor).astype(out[name].dtype)
    return out
```

```python
import math
from contextlib import ExitStack

import numpy as np

import concourse.bass as bass
from concourse import mybir

F32 = mybir.dt.float32
F32R = mybir.dt.float32r
U8 = mybir.dt.uint8
ALU = mybir.AluOpType
ACT = mybir.ActivationFunctionType
AX_X = mybir.AxisListType.X

P = 128
D = 2048
KT = D // P
L = 256
MT = L // P
N = 512
RH, RDK = 4, 256
GH, GDK, GDV = 4, 128, 256
LOW = 16
D_FF = ((8 * D // 3 + 255) // 256) * 256
C_RK, C_RV, C_GK, C_GV, C_GA = 0, 1024, 2048, 2560, 3584
C_RQ, C_RG, C_GQ, C_GG, C_GATE_A = 3616, 4640, 5664, 6176, 7200
D_IN = 11296
EPS = 1e-6
GATE_NORM = 16.0

CTX_BLOCKS = C_GA // N
LAT_BLOCKS = (D_IN - C_RQ) // N
FF_BLOCKS = D_FF // N
OUT_BLOCKS = D // N
RAW, SPLIT = 8, 4
MOD_BLOCKS = 8
MOD_SLOTS = MOD_BLOCKS * 8
LEVELS = [1, 2, 4, 8, 16, 32, 64, 128]


def constants():
    f = np.float32
    n_f = RDK // 4
    inv = (f(10000.0) ** (-np.arange(n_f, dtype=f) / f(n_f))).astype(f)
    t = np.arange(L)
    ang = np.concatenate([(t // 64).astype(f)[:, None] * inv, (t % 64).astype(f)[:, None] * inv], axis=-1)
    rope = np.stack([np.cos(ang), np.sin(ang)], axis=1).astype(f)
    rope = rope.reshape(MT, P, 2, P).transpose(1, 2, 0, 3)
    s = np.arange(L)[:, None]
    before = (s < np.arange(L + 1)[None, :]).astype(f).reshape(MT, P, L + 1).transpose(1, 0, 2)
    after = (s > np.arange(L)[None, :]).astype(f).reshape(MT, P, L).transpose(1, 0, 2)
    i = np.arange(L)[None, :]
    delta = i - s
    dist = np.stack([np.maximum(delta, 0), np.maximum(-delta, 0), i + L - s, L - i + s], axis=0).astype(f)
    dist = dist.reshape(4, MT, P, L).transpose(2, 0, 1, 3)
    a, b = np.arange(P)[:, None], np.arange(P)[None, :]
    mask = np.stack([((a // h != b // h) & (a // (2 * h) == b // (2 * h))) for h in LEVELS[:-1]], axis=1)
    return {"k_ident": np.eye(P, dtype=f), "k_rope": np.ascontiguousarray(rope),
            "k_before": np.ascontiguousarray(before), "k_after": np.ascontiguousarray(after),
            "k_dist": np.ascontiguousarray(dist),
            "k_mask": np.ascontiguousarray(mask.astype(f))}


def build(nc, x, c, ctx_in, c_ctx, w_mod, b_mod, norm_mix_pre, norm_mix_post, norm_ffn_pre, norm_ffn_post,
          w_in, ret_decay, gla_a_up, gla_a_bias, ret_gn, gla_gn, w_up_ret, w_up_gla, w_out,
          ffn_w_gate, ffn_w_up, ffn_w_down, k_ident, k_rope, k_before, k_after, k_dist, k_mask, out):
    px = nc.dram_tensor("px", (L, D_IN), F32, kind="Internal").ap()
    pc = nc.dram_tensor("pc", (L, C_GA), F32, kind="Internal").ap()
    kwd = nc.dram_tensor("kwd", (2, L, GH * GDK), F32, kind="Internal").ap()
    gwd = nc.dram_tensor("gwd", (2, D), F32, kind="Internal").ap()
    hsd = nc.dram_tensor("hsd", (L, D), F32, kind="Internal").ap()

    with ExitStack() as ctx:
        cursor = [(nc.sbuf_base + 31) // 32 * 32]

        def at(name, shape, dt, offset):
            return nc.alloc_sbuf_tensor_at(name, shape, dt, offset=offset)

        def keep(name, shape, dt=F32):
            size = math.prod(shape[1:]) * (4 if dt != mybir.dt.uint8 else 1)
            off = cursor[0]
            cursor[0] += (size + 31) // 32 * 32
            return at(name, shape, dt, off)

        sems = {}

        def S(name):
            if name not in sems:
                sems[name] = ctx.enter_context(nc.semaphore(name))
            return sems[name]

        raw = keep("raw", [P, RAW, 2, N])
        w_hi = keep("w_hi", [P, SPLIT, 2, N], F32R)
        w_lo = keep("w_lo", [P, SPLIT, 2, N], F32R)
        h_off = cursor[0]
        h_hi = keep("h_hi", [P, KT, L], F32R)
        h_lo = keep("h_lo", [P, KT, L], F32R)
        stage_off = cursor[0]
        stage = keep("stage", [P, 4, N])
        ident = keep("ident", [P, P])
        ones = keep("ones", [P, 1])
        rope = keep("rope", [P, 2, MT, P])
        before = keep("before", [P, MT, L + 1])
        after = keep("after", [P, MT, L])
        rows = keep("rows", [P, P])
        cols = keep("cols", [P, 112])
        cols2 = keep("cols2", [P, 96])
        gw_cols = keep("gw_cols", [P, 2, KT])
        gw_rows = keep("gw_rows", [2 * KT, P])
        csil = keep("csil", [P, 2 * KT])
        mod_t = keep("mod_t", [P, 32, 2])
        scale1 = keep("scale1", [P, 2, KT])
        mod2 = keep("mod2", [P, 2, KT])
        lg = keep("lg", [P, 2 * RH])
        mask = keep("mask", [P, 7, P], U8)
        spare = keep("spare", [P, 16])
        ssq = keep("ssq", [P, 4])
        rstd = keep("rstd", [P, 4])
        minus_half = keep("minus_half", [P, 4])
        ssy = keep("ssy", [P, MT, OUT_BLOCKS])
        stats = keep("stats", [P, 2, MT, 6])
        mv = keep("mv", [P, 2, MT, 2])
        hr = keep("hr", [P, 2, MT, 1])
        base = cursor[0]
        K = 1024

        def reg(name, shape, kb, dt=F32):
            return at(name, shape, dt, base + kb * K)

        xn = at("xn", [P, 4, D], F32, h_off)
        xr_t = reg("xr_t", [P, KT, 4 * P], 0)
        acc = reg("acc", [P, 4, D], 0)
        hc_hi = reg("hc_hi", [P, KT, L], 32, F32R)
        hc_lo = reg("hc_lo", [P, KT, L], 48, F32R)
        mask_f = reg("mask_f", [P, 7, P], 88)
        rows2 = reg("rows2", [96, P], 92)
        junk0 = reg("junk0", [P, D], 32)
        mod_row = reg("mod_row", [2, MOD_BLOCKS, N], 64)
        wm = reg("wm", [P, 2, D], 64)
        ga_w = reg("ga_w", [P, KT, 2 * LOW], 80)
        ga_hi = reg("ga_hi", [P, KT, 2 * LOW], 82, F32R)
        ga_lo = reg("ga_lo", [P, KT, 2 * LOW], 84, F32R)
        ga_n = reg("ga_n", [P, 4, 2 * LOW], 86)
        la = reg("la", [P, 2, 4, GH * GDK], 32)
        cum = reg("cum", [P, 2, GH, L + 1], 48)
        dmat = reg("dmat", [P, RH, 4, L], 57)
        dist = reg("dist", [P, 4, MT, L], 73)
        kw = reg("kw", [P, 2, MT, GH * GDK], 81)
        gkc = reg("gkc", [P, MT, GH * GDK], 89)
        al_t = reg("al_t", [2 * LOW + 1, 4 * P], 57)
        a_up = reg("a_up", [2 * LOW + 1, 2, GH * GDK], 59)
        d_tmp = reg("d_tmp", [P, MT, L], 85)
        d_ctx = reg("d_ctx", [P, 2, MT, L], 81)
        r_q = reg("r_q", [P, MT, RDK], 0)
        r_k = reg("r_k", [P, MT, RDK], 2)
        r_kc = reg("r_kc", [P, MT, RDK], 4)
        r_v = reg("r_v", [P, 4, RDK], 6)
        r_g = reg("r_g", [P, MT, RDK], 10)
        r_tmp = reg("r_tmp", [P, 4, MT, P], 12)
        r_qt = reg("r_qt", [P, 2, L], 16)
        r_kt = reg("r_kt", [P, 4, L], 18)
        r_a = reg("r_a", [P, 4, L], 22)
        g_q = reg("g_q", [P, MT, GDK], 26)
        g_k = reg("g_k", [P, MT, GDK], 27)
        g_kw = reg("g_kw", [P, 2, MT, GDK], 28)
        g_v = reg("g_v", [P, 4, GDV], 30)
        g_g = reg("g_g", [P, MT, GDV], 34)
        g_qkt = reg("g_qkt", [P, 2, L], 36)
        g_arg = reg("g_arg", [P, 2, 4, L], 38)
        g_st = reg("g_st", [P, 2, L], 46)
        g_a = reg("g_a", [P, 4, P], 89)
        g_s = reg("g_s", [P, 2, GDV], 91)
        o_t = reg("o_t", [P, 2, 8, L], 73)
        o_hi = reg("o_hi", [P, 2, 8, L], 0, F32R)
        o_lo = reg("o_lo", [P, 2, 8, L], 16, F32R)
        gate_s = reg("gate_s", [P, 2, MT, N], 32)
        up_t = reg("up_t", [P, 2, MT, N], 40)
        mg = reg("mg", [P, MT, N], 48)
        y = reg("y", [P, MT, D], 54)
        hs = reg("hs", [P, MT, D], 0)
        g1w = reg("g1w", [P, D], 16)
        junk = reg("junk", [P, D], 24)
        h2n = reg("h2n", [P, MT, D], 32)
        h2f = reg("h2f", [P, 2, 2, L], 48)
        hid_hi = reg("hid_hi", [P, FF_BLOCKS * 4, L], 0, F32R)
        hid_lo = reg("hid_lo", [P, FF_BLOCKS * 4, L], 44, F32R)
        hid_n = reg("hid_n", [P, MT, N], 88)
        sg = at("sg", [P, MT, N], F32, stage_off)
        g2w = at("g2w", [P, D], F32, stage_off)
        y2 = at("y2", [P, MT, D], F32, h_off)
        hs2 = at("hs2", [P, MT, D], F32, h_off + 16 * K)
        junk2 = reg("junk2", [P, N], 88)
        assert base + 93 * K <= nc.sbuf_usable_end, (base, nc.sbuf_usable_end)

        ps = ctx.enter_context(nc.psum_tensor("ps", [P, 8, N], F32))
        psf = ps[:, :, :].rearrange("p b n -> p (b n)")

        def bank(b, n=1):
            return psf[:, b * N:(b + n) * N]

        landed = [S(f"raw_landed{j}") for j in range(RAW)]
        mod_used, w_high, w_low, w_used = S("mod_slot_used"), S("w_high_ready"), S("w_low_ready"), S("w_slot_used")
        staged = [S(f"stage_written{b}") for b in range(4)]
        stored = [S(f"stage_stored{b}") for b in range(4)]

        w_in_k = w_in.rearrange("(k p) n -> p k n", p=P)
        w_mod_k = w_mod.rearrange("(k p) n -> p k n", p=P)
        w_ur_k = w_up_ret.rearrange("(k p) n -> p k n", p=P)
        w_ug_k = w_up_gla.rearrange("(k p) n -> p k n", p=P)
        w_out_k = w_out.rearrange("(k p) n -> p k n", p=P)
        w_fg_k = ffn_w_gate.rearrange("(k p) n -> p k n", p=P)
        w_fu_k = ffn_w_up.rearrange("(k p) n -> p k n", p=P)
        w_fd_k = ffn_w_down.rearrange("(k p) n -> p k n", p=P)
        px_t = px.rearrange("(m p) n -> p m n", p=P)
        pc_t = pc.rearrange("(m p) n -> p m n", p=P)

        S_CTX = 0
        S_LAT = S_CTX + 8 * CTX_BLOCKS
        S_UP = S_LAT + 8 * LAT_BLOCKS
        S_OUT = S_UP + 8 * OUT_BLOCKS
        S_FFN = S_OUT + 8 * OUT_BLOCKS
        DOWN_SLOTS = D_FF // P // 2
        S_DOWN = S_FFN + 16 * FF_BLOCKS

        block = ctx.enter_context(nc.Block())

        @block.sync
        def _(sp):
            def slot(s, j, src, k, col):
                q = j % RAW
                if isinstance(s, int) and s + j < RAW:
                    sp.wait_ge(mod_used, MOD_SLOTS - RAW + s + j + 1)
                else:
                    sp.wait_ge(w_low, s + (j - RAW + 1))
                sp.dma_start(raw[:, q, :, :], src[:, k:k + 2, bass.ds(col, N)]).then_inc(landed[q], 16)

            for n in range(MOD_BLOCKS):
                for j in range(8):
                    if n > 0:
                        sp.wait_ge(mod_used, 8 * n + j - RAW + 1)
                    sp.dma_start(raw[:, j, :, :], w_mod_k[:, 2 * j:2 * j + 2, n * N:(n + 1) * N]).then_inc(landed[j], 16)
            for j in range(8):
                slot(0, j, w_in_k, 2 * j, 0)
            for j in range(8):
                slot(8, j, w_in_k, 2 * j, N)
            with sp.Fori(0, (CTX_BLOCKS - 3) // 2) as i:
                for u in range(2):
                    for j in range(8):
                        slot(i * 16 + (16 + 8 * u), j, w_in_k, 2 * j, i * (2 * N) + (2 + u) * N)
            for j in range(8):
                slot(48, j, w_in_k, 2 * j, 6 * N)
            for t in range(3):
                for j in range(8):
                    slot(S_LAT + 8 * t, j, w_in_k, 2 * j, C_RQ + t * N)
            with sp.Fori(0, 6) as i:
                for u in range(2):
                    for j in range(8):
                        slot(i * 16 + (S_LAT + 8 * (3 + u)), j, w_in_k, 2 * j, i * (2 * N) + (C_RQ + (3 + u) * N))
            with sp.Fori(0, OUT_BLOCKS) as i:
                for j in range(8):
                    slot(i * 8 + S_UP, j, w_ur_k if j < 4 else w_ug_k, 2 * (j % 4), i * N)
            with sp.Fori(0, OUT_BLOCKS) as i:
                for j in range(8):
                    slot(i * 8 + S_OUT, j, w_out_k, 2 * j, i * N)
            with sp.Fori(0, FF_BLOCKS) as i:
                for j in range(16):
                    slot(i * 16 + S_FFN, j, w_fg_k if j < 8 else w_fu_k, 2 * (j % 8), i * N)
            for n in range(OUT_BLOCKS):
                for j in range(DOWN_SLOTS):
                    s = S_DOWN + n * DOWN_SLOTS + j
                    sp.wait_ge(w_low, s - RAW + 1)
                    sp.dma_start(raw[:, s % RAW, :, :], w_fd_k[:, 2 * j:2 * j + 2, n * N:(n + 1) * N])\
                      .then_inc(landed[s % RAW], 16)
            for m in range(MT):
                for n in range(OUT_BLOCKS):
                    sp.wait_ge(S("final_ready"), OUT_BLOCKS * m + n + 1)
                    sp.dma_start(out[m * P:(m + 1) * P, n * N:(n + 1) * N], y2[:, m, n * N:(n + 1) * N])\
                      .then_inc(S("out_stored"), 16)
            sp.wait_ge(S("out_stored"), 16 * MT * OUT_BLOCKS)

        @block.gpsimd
        def _(pool):
            r0 = 0
            for v, n in ((c, 16), (c_ctx, 16), (norm_mix_pre, 16), (norm_ffn_pre, 16), (ret_gn, 8), (gla_gn, 8),
                         (b_mod[0:2 * D], 32)):
                pool.dma_start(rows[r0:r0 + n, :], v.rearrange("(r q) -> r q", q=P)).then_inc(S("rows_landed"), 16)
                r0 += n
            for r0, n, v in ((0, 64, b_mod[2 * D:6 * D]), (64, 16, norm_mix_post), (80, 16, norm_ffn_post)):
                pool.dma_start(rows2[r0:r0 + n, :], v.rearrange("(r q) -> r q", q=P)).then_inc(S("rows_landed"), 16)
            pool.dma_start(ident[:, :], k_ident).then_inc(S("rows_landed"), 16)
            for m in range(4):
                src = x if m < 2 else ctx_in
                pool.dma_start(xn[:, m, :], src[(m % 2) * P:(m % 2 + 1) * P, :]).then_inc(S(f"x_landed{m}"), 16)
            pool.dma_start(lg[:, :], ret_decay.rearrange("(a d) h -> a (d h)", a=1).broadcast_to([P, 2 * RH]))\
                .then_inc(S("consts_landed"), 16)
            for t, k in ((rope, k_rope), (before, k_before), (after, k_after)):
                pool.dma_start(t[:, :, :] if t is not rope else t[:, :, :, :], k).then_inc(S("consts_landed"), 16)
            pool.dma_start(mask_f[:, :, :], k_mask).then_inc(S("consts_landed"), 16)
            pool.memset(ones[:, :], 1.0).then_inc(S("ones_ready"), 1)
            pool.memset(minus_half[:, :], -0.5).then_inc(S("ones_ready"), 1)
            pool.wait_ge(S("ones_ready"), 2)
            pool.wait_ge(S("ssq_ready"), 1)
            pool.tensor_tensor(rstd[:, :], ssq[:, :], minus_half[:, :], ALU.pow).then_inc(S("rstd_ready"), 1)

            pool.dma_start(ga_w[:, :, :], w_in_k[:, :, C_GA:C_GA + 2 * LOW]).then_inc(S("ga_landed"), 16)

            pool.wait_ge(S("ga_done"), 1)
            pool.memset(a_up[:, :, :], 0.0).then_inc(S("gate_rows_set"), 1)
            pool.memset(al_t[:, :], 1.0).then_inc(S("gate_rows_set"), 1)
            pool.wait_ge(S("gate_rows_set"), 2)
            for d in range(2):
                pool.dma_start(a_up[d * LOW:(d + 1) * LOW, d, :], gla_a_up[d]).then_inc(S("a_up_landed"), 16)
            pool.dma_start(a_up[2 * LOW:2 * LOW + 1, :, :], gla_a_bias.rearrange("(a d) n -> a d n", a=1))\
                .then_inc(S("a_up_landed"), 16)
            for m in range(4):
                pool.wait_ge(stored[m], 16 * 5)
            pool.dma_start(gkc[:, :, :], pc_t[:, :, C_GK:C_GK + GH * GDK]).then_inc(S("gkc_landed"), 16)
            for d in range(2):
                pool.wait_ge(S("kw_ready"), d + 1)
                pool.dma_start(kwd[d].rearrange("(m p) n -> p m n", p=P), kw[:, d, :, :]).then_inc(S("kw_stored"), 16)
            pool.wait_ge(S("wm_used"), 4 * KT)
            pool.dma_start(dist[:, :, :, :], k_dist).then_inc(S("dist_landed"), 16)
            pool.wait_ge(S("lg_exp"), 1)
            pool.tensor_scalar(lg[:, :], lg[:, :], -1.0, None, ALU.mult).then_inc(S("lg_ready"), 1)
            pool.wait_ge(S("lg_ready"), 1)
            pool.wait_ge(S("dist_landed"), 16)
            pool.wait_ge(S("kw_stored"), 32)
            for h in range(RH):
                if h > 0:
                    pool.wait_ge(S("dist_sum"), h)
                pool.tensor_scalar(d_tmp[:, :, :], dist[:, 1, :, :], lg[:, RH + h:RH + h + 1], None, ALU.mult)\
                    .then_inc(S("dist_part"), 1)
                pool.tensor_scalar(dmat[:, h, 2:4, :], dist[:, 0, :, :], lg[:, h:h + 1], None, ALU.mult)\
                    .then_inc(S("dist_part"), 1)
                pool.wait_ge(S("dist_part"), 2 * h + 2)
                pool.tensor_tensor(dmat[:, h, 2:4, :], dmat[:, h, 2:4, :], d_tmp[:, :, :], ALU.add)\
                    .then_inc(S("dist_sum"), 1)
            for h in range(RH):
                pool.wait_ge(S("dctx_exp"), h + 1)
                pool.tensor_tensor(dmat[:, h, 0:2, :], dmat[:, h, 0:2, :], d_ctx[:, h % 2, :, :], ALU.add)\
                    .then_inc(S("dctx_ready"), 1)
            pool.wait_ge(S("gw_rows_ready"), 1)
            pool.dma_start(gwd.rearrange("d (r q) -> (d r) q", q=P), gw_rows[:, :]).then_inc(S("gw_stored"), 16)

            pool.wait_ge(stored[0], 16 * 10)
            pool.wait_ge(stored[1], 16 * 10)
            pool.wait_ge(stored[2], 16 * 10)
            pool.wait_ge(stored[3], 16 * 10)
            pool.wait_ge(S("kw_stored"), 32)
            pool.wait_ge(S("gw_stored"), 16)
            pool.wait_ge(S("dctx_ready"), RH)
            with pool.Fori(0, RH) as i:
                rc, gc = i * RDK, i * GDK
                pool.wait_ge(S("ret_head_done"), i + 1)
                pool.wait_ge(S("gla_head_done"), i + 1)
                pool.dma_start(g_q[:, :, :], px_t[:, :, bass.ds(gc + C_GQ, GDK)]).then_inc(S("g_qk_landed"), 16)
                pool.dma_start(g_k[:, :, :], px_t[:, :, bass.ds(gc + C_GK, GDK)]).then_inc(S("g_qk_landed"), 16)
                pool.dma_start(r_q[:, :, :], px_t[:, :, bass.ds(rc + C_RQ, RDK)]).then_inc(S("r_qk_landed"), 16)
                pool.dma_start(r_k[:, :, :], px_t[:, :, bass.ds(rc + C_RK, RDK)]).then_inc(S("r_qk_landed"), 16)
                pool.dma_start(r_kc[:, :, :], pc_t[:, :, bass.ds(rc + C_RK, RDK)]).then_inc(S("r_kc_landed"), 16)
                for d in range(2):
                    pool.dma_start(g_kw[:, d, :, :],
                                   kwd[d].rearrange("(m p) n -> p m n", p=P)[:, :, bass.ds(gc, GDK)])\
                        .then_inc(S("g_v_landed"), 16)
                pool.dma_start(g_v[:, 0:2, :], pc_t[:, :, bass.ds(rc + C_GV, GDV)]).then_inc(S("g_v_landed"), 16)
                pool.dma_start(g_v[:, 2:4, :], px_t[:, :, bass.ds(rc + C_GV, GDV)]).then_inc(S("g_v_landed"), 16)
                pool.dma_start(r_v[:, 0:2, :], pc_t[:, :, bass.ds(rc + C_RV, RDK)]).then_inc(S("r_v_landed"), 16)
                pool.dma_start(r_v[:, 2:4, :], px_t[:, :, bass.ds(rc + C_RV, RDK)]).then_inc(S("r_v_landed"), 16)
                pool.dma_start(r_g[:, :, :], px_t[:, :, bass.ds(rc + C_RG, RDK)]).then_inc(S("gates_landed"), 16)
                pool.wait_ge(stored[0], i * 16 + 160)
                pool.wait_ge(stored[1], i * 16 + 160)
                pool.dma_start(g_g[:, :, :], px_t[:, :, bass.ds(rc + C_GG, GDV)]).then_inc(S("gates_landed"), 16)
                pool.wait_ge(S("r_qk_landed"), i * 32 + 32)
                for n, t in enumerate((r_q, r_k)):
                    a, b = t[:, :, 0:P], t[:, :, P:2 * P]
                    for e, (u, f) in enumerate(((a, 0), (b, 1), (a, 1), (b, 0))):
                        pool.tensor_tensor(r_tmp[:, e, :, :], u, rope[:, f, :, :], ALU.mult)\
                            .then_inc(S("rope_prod"), 1)
                    pool.wait_ge(S("rope_prod"), i * 8 + (4 * n + 4))
                    pool.tensor_tensor(a, r_tmp[:, 0, :, :], r_tmp[:, 1, :, :], ALU.subtract).then_inc(S("rope_ready"), 1)
                    pool.tensor_tensor(b, r_tmp[:, 2, :, :], r_tmp[:, 3, :, :], ALU.add).then_inc(S("rope_ready"), 1)
                    pool.wait_ge(S("rope_ready"), i * 4 + 2 * n + 2)
                pool.wait_ge(S("g_ms_ready"), i + 1)
                pool.tensor_tensor(hr[:, 1, :, :], mv[:, 1, :, 0:1], minus_half[:, 0:MT].rearrange("p (m o) -> p m o", o=1), ALU.pow)\
                    .then_inc(S("g_rstd_ready"), 1)
                pool.wait_ge(S("r_var_ready"), i + 1)
                pool.tensor_tensor(hr[:, 0, :, :], mv[:, 0, :, 1:2], minus_half[:, 0:MT].rearrange("p (m o) -> p m o", o=1), ALU.pow)\
                    .then_inc(S("r_rstd_ready"), 1)

            pool.wait_ge(S("gla_head_done"), RH + 1)
            pool.wait_ge(S("ret_head_done"), RH + 1)

            pool.wait_ge(stored[2], 16 * 12)
            pool.wait_ge(stored[3], 16 * 12)
            pool.wait_ge(stored[0], 16 * 14)
            pool.wait_ge(stored[1], 16 * 14)
            pool.dma_start(gate_s[:, 0, :, :], px_t[:, :, C_GATE_A:C_GATE_A + N]).then_inc(S("gate_landed0"), 16)
            pool.dma_start(gate_s[:, 1, :, :], px_t[:, :, C_GATE_A + D:C_GATE_A + D + N]).then_inc(S("gate_landed1"), 16)
            pool.wait_ge(stored[2], 16 * 14)
            pool.wait_ge(stored[3], 16 * 14)
            pool.wait_ge(stored[0], 16 * 15)
            pool.wait_ge(stored[1], 16 * 15)
            with pool.Fori(0, OUT_BLOCKS - 1) as i:
                for g in range(2):
                    pool.wait_ge(S(f"gate_used{g}"), i + 1)
                    pool.dma_start(gate_s[:, g, :, :], px_t[:, :, bass.ds(i * N + (C_GATE_A + g * D + N), N)])\
                        .then_inc(S(f"gate_landed{g}"), 16)
            pool.wait_ge(w_used, S_OUT)
            pool.dma_start(hs[:, :, :], x.rearrange("(m p) n -> p m n", p=P)).then_inc(S("res_landed"), 16)
            pool.dma_start(g1w[:, :], gwd[0:1, :].broadcast_to([P, D])).then_inc(S("res_landed"), 16)
            pool.wait_ge(S("ssy_ready"), 2)
            pool.tensor_tensor(rstd[:, 0:MT], ssq[:, 0:MT], minus_half[:, 0:MT], ALU.pow).then_inc(S("rstd_ready"), 1)
            for m in range(MT):
                pool.wait_ge(S("hs_ready"), m + 1)
                pool.dma_start(hsd[m * P:(m + 1) * P, :], hs[:, m, :]).then_inc(S("hs_stored"), 16)
            pool.wait_ge(S("ssh_ready"), 1)
            pool.tensor_tensor(rstd[:, 2:4], ssq[:, 2:4], minus_half[:, 0:MT], ALU.pow).then_inc(S("rstd_ready"), 1)
            pool.wait_ge(S("hs_stored"), 16 * MT)
            pool.wait_ge(w_used, S_DOWN)
            pool.wait_ge(S("hid_n_ready"), FF_BLOCKS)
            pool.dma_start(hs2[:, :, :], hsd.rearrange("(m p) n -> p m n", p=P)).then_inc(S("end_landed"), 16)
            pool.dma_start(g2w[:, :], gwd[1:2, :].broadcast_to([P, D])).then_inc(S("end_landed"), 16)
            pool.wait_ge(S("ssy_ready"), 4)
            pool.tensor_tensor(rstd[:, 0:MT], ssq[:, 0:MT], minus_half[:, 0:MT], ALU.pow).then_inc(S("rstd_ready"), 1)

        def chunk_of(n):
            return n // KT, n % KT

        @block.scalar
        def _(act):
            def split(s, j):
                if isinstance(s, int):
                    s, j = 0, s + j
                    act.wait_ge(landed[j % RAW], 16 * ((j + MOD_SLOTS) // RAW + 1))
                else:
                    act.wait_ge(landed[j % RAW], s * 2 + 16 * ((j + MOD_SLOTS) // RAW + 1))
                if not isinstance(s, int) or j >= SPLIT:
                    act.wait_ge(w_used, s + (j - SPLIT + 1))
                act.activation(w_hi[:, j % SPLIT, :, :], raw[:, j % RAW, :, :], ACT.Copy).then_inc(w_high, 1)

            def stage_ctx(b, group):
                act.wait_ge(w_used, b * 8 + 8)
                for m in range(4):
                    if not isinstance(b, int) or b > 0:
                        act.wait_ge(stored[m], b * 16)
                    act.activation(stage[:, m, :], bank(4 * group + m), ACT.Copy).then_inc(staged[m], 1)

            def store_ctx(b):
                for m in range(4):
                    act.wait_ge(staged[m], b + 1)
                    act.dma_start((px if m < 2 else pc)[m % 2 * P:(m % 2 + 1) * P, bass.ds(b * N, N)], stage[:, m, :])\
                        .then_inc(stored[m], 16)

            def store_lat(i, t):
                for m in range(2):
                    b = 2 * (t % 2) + m
                    act.wait_ge(staged[b], i + (CTX_BLOCKS + t // 2 + 1))
                    act.dma_start(px[m * P:(m + 1) * P, bass.ds(i * (2 * N) + (C_RQ + t * N), N)], stage[:, b, :])\
                        .then_inc(stored[b], 16)

            def stage_lat(i, t):
                act.wait_ge(w_used, i * 16 + (S_LAT + 8 * (t + 1)))
                for m in range(2):
                    b = 2 * (t % 2) + m
                    act.wait_ge(stored[b], i * 16 + 16 * (CTX_BLOCKS + t // 2))
                    act.activation(stage[:, b, :], bank(b), ACT.Copy).then_inc(staged[b], 1)

            def load_chunk(i, n, g, k):
                if not isinstance(i, int) or n >= 2:
                    act.wait_ge(S("wm_used"), i * 16 + (n - 1))
                act.dma_start(wm[:, n % 2, :], w_mod_k[:, k, bass.ds(i * D + (2 + g) * D, D)])\
                    .then_inc(S(f"wm_landed{n % 2}"), 16)

            act.wait_ge(S("cols_turned"), 1)
            act.activation(csil[:, :], bank(7)[:, 0:2 * KT], ACT.Silu).then_inc(S("cols_ready"), 1)
            act.activation(cols[:, :], bank(7)[:, 0:112], ACT.Copy).then_inc(S("cols_ready"), 1)
            act.activation(cols2[:, :], bank(7)[:, 128:224], ACT.Copy).then_inc(S("cols_ready"), 1)
            for m in range(4):
                act.wait_ge(S(f"x_landed{m}"), 16)
                if m > 0:
                    act.wait_ge(S("square"), m)
                act.activation(junk0[:, :], xn[:, m, :], ACT.Square, accum_out=ssq[:, m:m + 1]).then_inc(S("square"), 1)
            act.wait_ge(S("consts_landed"), 16 * 5)
            act.activation(lg[:, :], lg[:, :], ACT.Exp).then_inc(S("lg_exp"), 1)
            act.wait_ge(S("rstd_ready"), 1)
            for m in range(4):
                act.activation(xn[:, m, :], xn[:, m, :], ACT.Copy, scale=rstd[:, m:m + 1]).then_inc(S("x_scaled"), 1)
            for n in range(MOD_BLOCKS):
                act.wait_ge(mod_used, 8 * n + 8)
                act.activation(mod_row[:, n, :], bank(n % 2)[0:2, :], ACT.Copy).then_inc(S("mod_row_ready"), 1)

            for j in range(8):
                for k in (2 * j, 2 * j + 1):
                    act.wait_ge(S("h1_ready"), 2 * k + 2)
                    act.activation(h_hi[:, k, :], xr_t[:, k, 0:L], ACT.Copy).then_inc(S("h1_hi"), 1)
                    act.activation(hc_hi[:, k, :], xr_t[:, k, L:2 * L], ACT.Copy).then_inc(S("h1_hi"), 1)
                split(0, j)
            act.wait_ge(S("mod_cols_done"), 1)
            load_chunk(0, 0, 0, 0)
            for j in range(8):
                if j == 4:
                    stage_ctx(0, 0)
                if j == 5:
                    store_ctx(0)
                split(8, j)
                load_chunk(0, j + 1, 0, j + 1)
            with act.Fori(0, 2) as i:
                for u in range(2):
                    for j in range(8):
                        if j == 4:
                            stage_ctx(i * 2 + (1 + u), 1 - u)
                        if j == 5:
                            store_ctx(i * 2 + (1 + u))
                        split(i * 16 + (16 + 8 * u), j)
                        n = 8 + 8 * u + j + 1
                        load_chunk(i, n, *chunk_of(n))
            for j in range(8):
                if j == 4:
                    stage_ctx(5, 1)
                if j == 5:
                    store_ctx(5)
                split(48, j)
                load_chunk(0, 40 + j + 1, *chunk_of(40 + j + 1))
            act.wait_ge(S("ga_landed"), 16)
            act.activation(ga_hi[:, :, :], ga_w[:, :, :], ACT.Copy).then_inc(S("ga_hi_ready"), 1)

            def at_pre(p):
                if p == 4:
                    act.wait_ge(S("ga_turned"), 1)
                    act.wait_ge(S("gate_rows_set"), 2)
                    act.activation(al_t[0:2 * LOW, :], bank(4)[0:2 * LOW, :], ACT.Copy).then_inc(S("al_ready"), 1)
                if p in (5, 7):
                    d = (p - 5) // 2
                    z = bank(4, 4)
                    t = la[:, d, :, :].rearrange("p m n -> p (m n)")
                    act.wait_ge(S("z_done"), d + 1)
                    act.activation(t, z, ACT.Abs).then_inc(S("la_step"), 1)
                    act.wait_ge(S("la_step"), 3 * d + 1)
                    act.activation(t, t, ACT.Exp, scale=-1.0).then_inc(S("la_step"), 1)
                    act.wait_ge(S("la_step"), 3 * d + 2)
                    act.activation(t, t, ACT.Ln, bias=1.0).then_inc(S("la_step"), 1)
                if p in (9, 10):
                    d = p - 9
                    act.wait_ge(S("sums_done"), d + 1)
                    act.activation(cum[:, d, :, :], bank(4, 4).rearrange("p (h n) -> p h n", h=GH)[:, :, 0:L + 1],
                                   ACT.Copy).then_inc(S("cum_ready"), 1)
                if p in (12, 13):
                    d = p - 12
                    act.wait_ge(S("ctx_sums_done"), d + 1)
                    act.activation(kw[:, d, :, :], bank(4 + 2 * d, 2).rearrange("p (m n) -> p m n", m=MT), ACT.Exp,
                                   scale=1.0 / GATE_NORM).then_inc(S("kw_exp"), 1)
                if p == 19:
                    act.wait_ge(S("gw_turned"), 1)
                    act.activation(gw_rows[:, :], bank(5)[0:2 * KT, 0:P], ACT.Copy).then_inc(S("gw_rows_ready"), 1)

            for t in range(3):
                for j in range(8):
                    if j == 4 and t == 0:
                        stage_ctx(6, 0)
                    if j == 1 and t == 0:
                        act.wait_ge(S("ga_done"), 1)
                        act.activation(ga_n[:, :, :], bank(4)[:, 0:8 * LOW].rearrange("p (m n) -> p m n", m=4), ACT.Copy)\
                            .then_inc(S("ga_n_ready"), 1)
                    if j == 5 and t == 0:
                        store_ctx(6)
                    if j == 4 and t > 0:
                        stage_lat(0, t - 1)
                    if j == 5 and t > 0:
                        store_lat(0, t - 1)
                    at_pre(8 * t + j)
                    split(S_LAT + 8 * t, j)
                    n = 48 + 8 * t + j + 1
                    if n < 4 * KT:
                        load_chunk(0, n, *chunk_of(n))
            with act.Fori(0, 2) as i:
                for u in range(2):
                    for j in range(8):
                        if j == 4:
                            stage_lat(i, 2 + u)
                        if j == 5:
                            store_lat(i, 2 + u)
                        split(i * 16 + (S_LAT + 24 + 8 * u), j)
            act.wait_ge(S("kw_stored"), 32)
            for h in range(RH):
                act.wait_ge(S("dist_sum"), h + 1)
                act.activation(dmat[:, h, 2:4, :], dmat[:, h, 2:4, :], ACT.Exp)
                act.activation(dmat[:, h, 0:2, :], dist[:, 2, :, :], ACT.Exp, scale=lg[:, h:h + 1])
                if h >= 2:
                    act.wait_ge(S("dctx_ready"), h - 1)
                act.activation(d_ctx[:, h % 2, :, :], dist[:, 3, :, :], ACT.Exp, scale=lg[:, RH + h:RH + h + 1])\
                    .then_inc(S("dctx_exp"), 1)

            with act.Fori(0, RH) as i:
                for p in range(16):
                    if p in (4, 12):
                        stage_lat(i, 6 + (p - 4) // 8)
                    if p in (5, 13):
                        store_lat(i, 6 + (p - 4) // 8)
                    if p == 3:
                        act.wait_ge(S("gates_landed"), i * 32 + 32)
                        act.activation(r_g[:, :, :], r_g[:, :, :], ACT.Silu).then_inc(S("r_silu"), 1)
                        act.activation(g_g[:, :, :], g_g[:, :, :], ACT.Silu).then_inc(S("g_silu"), 1)
                    if p == 4:
                        act.wait_ge(S("g_arg_ready"), i * 2 + 1)
                        act.activation(g_arg[:, :, :, :], g_arg[:, :, :, :], ACT.Exp, scale=1.0 / GATE_NORM)\
                            .then_inc(S("g_exp_ready"), 1)
                        act.wait_ge(S("g_st_arg"), i + 1)
                        act.activation(g_st[:, 1, :], g_st[:, 1, :], ACT.Exp, scale=1.0 / GATE_NORM)\
                            .then_inc(S("g_st_exp"), 1)
                        act.activation(g_st[:, 0:1, :], cum[:, 0, bass.ds(i, 1), 1:L + 1], ACT.Exp, scale=1.0 / GATE_NORM)\
                            .then_inc(S("g_st_exp"), 1)
                    if p == 5:
                        act.wait_ge(S("g_qk_turned"), i + 1)
                        act.activation(g_qkt[:, 0, :], bank(6)[:, 0:L], ACT.Copy, scale=GDK ** -0.5)\
                            .then_inc(S("g_qkt_ready"), 1)
                        act.activation(g_qkt[:, 1, :], bank(6)[:, L:2 * L], ACT.Copy).then_inc(S("g_qkt_ready"), 1)
                    if p == 6:
                        act.wait_ge(S("g_state_done"), i + 1)
                        act.activation(g_s[:, :, :], bank(6).rearrange("p (d n) -> p d n", d=2), ACT.Copy)\
                            .then_inc(S("g_s_ready"), 1)
                        act.wait_ge(S("r_kc_turned"), i + 1)
                        act.activation(r_kt[:, 0:2, :], bank(4).rearrange("p (f n) -> p f n", f=2), ACT.Copy)\
                            .then_inc(S("r_kct_ready"), 1)
                    if p == 7:
                        act.wait_ge(S("g_arg_ready"), i * 2 + 2)
                        act.activation(g_arg[:, :, :, :], g_arg[:, :, :, :], ACT.Exp, scale=1.0 / GATE_NORM)\
                            .then_inc(S("g_exp_ready"), 1)
                    if p == 8:
                        act.wait_ge(S("r_qk_turned"), i + 1)
                        act.activation(r_qt[:, :, :], bank(5).rearrange("p (f n) -> p f n", f=2), ACT.Copy,
                                       scale=RDK ** -0.5).then_inc(S("r_qkt_ready"), 1)
                        act.activation(r_kt[:, 2:4, :], bank(4).rearrange("p (f n) -> p f n", f=2), ACT.Copy)\
                            .then_inc(S("r_qkt_ready"), 1)
                    if p == 9:
                        act.wait_ge(S("g_levels_done"), i * 2 + 2)
                        act.activation(g_a[:, 2:4, :], bank(7)[:, L:2 * L].rearrange("p (a n) -> p a n", a=2), ACT.Copy)\
                            .then_inc(S("g_cross_ready"), 1)
                    split(i * 16 + (S_LAT + 8 * 7), p)

            for g in range(2):
                act.wait_ge(S("ret_head_done" if g == 0 else "gla_head_done"), RH + 1)
                act.activation(o_hi[:, g, :, :], o_t[:, g, :, :], ACT.Copy).then_inc(S("o_hi_ready"), 1)

            def turn_merged(n):
                act.wait_ge(S("turned"), n + 1)
                act.activation(h_hi[:, bass.ds(n * 4, 4), :], bank(4, 2).rearrange("p (q n) -> p q n", q=4), ACT.Copy)\
                    .then_inc(S("turned_hi"), 1)

            def up_block(s, n, prev):
                for j in range(8):
                    if j == 4 and prev is None:
                        stage_lat(0, 14)
                    if j == 5 and prev is None:
                        store_lat(0, 14)
                    if j == 6 and prev is not None:
                        turn_merged(prev)
                    if j >= 6:
                        g = j - 6
                        act.wait_ge(S(f"gate_landed{g}"), n * 16 + 16)
                        act.activation(gate_s[:, g, :, :], gate_s[:, g, :, :], ACT.Sigmoid).then_inc(S(f"gate_ready{g}"), 1)
                    split(s, j)
            up_block(S_UP, 0, None)
            with act.Fori(0, OUT_BLOCKS - 1) as i:
                up_block(i * 8 + (S_UP + 8), i + 1, i)

            def take_y(n, yy, jk, slots, first):
                pair = 1 - n % 2
                act.wait_ge(w_used, slots)
                act.activation(yy[:, :, n * N:(n + 1) * N], bank(2 * pair, 2).rearrange("p (m n) -> p m n", m=MT), ACT.Copy)
                for m in range(MT):
                    if first + n + m > 0:
                        act.wait_ge(S("y_square"), 2 * (first + n) + m)
                    act.activation(jk[:, 0:N], bank(2 * pair + m), ACT.Square, accum_out=ssy[:, m, n:n + 1])\
                        .then_inc(S("y_square"), 1)

            for n in range(OUT_BLOCKS):
                for j in range(8):
                    if n == 0 and j == 6:
                        turn_merged(OUT_BLOCKS - 1)
                    if n > 0 and j == 4:
                        take_y(n - 1, y, junk, S_OUT + 8 * n, 0)
                    split(S_OUT + 8 * n, j)
            for j in range(4):
                split(S_FFN, j)
            take_y(OUT_BLOCKS - 1, y, junk, S_FFN, 0)
            for m in range(MT):
                act.wait_ge(S("hs_ready"), m + 1)
                act.wait_ge(S("square"), 4 + m)
                act.activation(junk[:, :], hs[:, m, :], ACT.Square, accum_out=ssq[:, 2 + m:3 + m]).then_inc(S("square"), 1)
            act.wait_ge(S("rstd_ready"), 3)
            for m in range(MT):
                act.activation(h2n[:, m, :], hs[:, m, :], ACT.Copy, scale=rstd[:, 2 + m:3 + m]).then_inc(S("h2n_ready"), 1)

            def turn_hidden(n):
                act.wait_ge(S("turned"), n + (OUT_BLOCKS + 1))
                act.activation(hid_hi[:, bass.ds(n * 4, 4), :], bank(4, 2).rearrange("p (q n) -> p q n", q=4), ACT.Copy)\
                    .then_inc(S("turned_hi"), 1)

            def ffn_block(s, n, prev):
                for j in range(16):
                    if prev is None and j < 8:
                        act.wait_ge(S("h2_turned"), j + 1)
                        if j >= 2:
                            act.wait_ge(S("h2_lo_ready"), j - 1)
                        for e in range(2):
                            k = 2 * j + e
                            act.activation(h2f[:, j % 2, e, :], bank(4 + j % 4)[:, e * L:(e + 1) * L], ACT.Identity,
                                           scale=mod2[:, 1, k:k + 1], bias=mod2[:, 0, k:k + 1]).then_inc(S("h2f_ready"), 1)
                        act.wait_ge(S("h2f_ready"), 2 * j + 2)
                        act.activation(h_hi[:, 2 * j:2 * j + 2, :], h2f[:, j % 2, :, :], ACT.Copy).then_inc(S("h2_hi_ready"), 1)
                    if prev is not None and j == 6:
                        turn_hidden(prev)
                    if j == 12:
                        act.wait_ge(w_used, n * 16 + (S_FFN + 8))
                        if prev is not None:
                            act.wait_ge(S("hid_n_ready"), n)
                        act.activation(sg[:, :, :], bank(2, 2).rearrange("p (m n) -> p m n", m=MT), ACT.Silu)\
                            .then_inc(S("silu_ready"), 1)
                    if prev is not None or j >= 4:
                        split(s, j)
            act.wait_ge(S("hs_stored"), 16 * MT)
            ffn_block(S_FFN, 0, None)
            with act.Fori(0, FF_BLOCKS - 1) as i:
                ffn_block(i * 16 + (S_FFN + 16), i + 1, i)
            for n in range(OUT_BLOCKS):
                for j in range(DOWN_SLOTS):
                    if n == 0 and j == 6:
                        turn_hidden(FF_BLOCKS - 1)
                    if n > 0 and j == 4:
                        take_y(n - 1, y2, junk2, S_DOWN + n * DOWN_SLOTS, OUT_BLOCKS)
                    split(S_DOWN + n * DOWN_SLOTS, j)
            take_y(OUT_BLOCKS - 1, y2, junk2, S_DOWN + OUT_BLOCKS * DOWN_SLOTS, OUT_BLOCKS)

        @block.vector
        def _(dve):
            def split(s, j):
                if isinstance(s, int):
                    s, j = 0, s + j
                dve.wait_ge(w_high, s + (j + 1))
                dve.tensor_tensor(w_lo[:, j % SPLIT, :, :], raw[:, j % RAW, :, :],
                                  w_hi[:, j % SPLIT, :, :].bitcast(F32), ALU.subtract).then_inc(w_low, 1)

            def add_chunk(i, n, g, k):
                b = n % 2
                a = acc[:, bass.ds(i + g, 1), :].rearrange("p o n -> p (o n)")
                dve.wait_ge(S(f"wm_landed{b}"), i * 128 + 16 * (n // 2 + 1))
                if k == 0:
                    dve.tensor_scalar(a, wm[:, b, :], csil[:, k:k + 1], None, ALU.mult).then_inc(S("wm_used"), 1)
                else:
                    dve.wait_ge(S("wm_used"), i * 16 + n)
                    dve.scalar_tensor_tensor(out=a, in0=wm[:, b, :], scalar=csil[:, k:k + 1], in1=a,
                                             op0=ALU.mult, op1=ALU.add).then_inc(S("wm_used"), 1)

            dve.memset(hr[:, 0, 0:1, :], 0.0).then_inc(S("ret_head_done"), 1)
            dve.memset(hr[:, 1, 0:1, :], 0.0).then_inc(S("gla_head_done"), 1)
            dve.wait_ge(S("consts_landed"), 16 * 5)
            dve.tensor_copy(mask[:, :, :], mask_f[:, :, :]).then_inc(S("mask_ready"), 1)
            dve.wait_ge(S("mask_ready"), 1)
            dve.wait_ge(S("square"), 4)
            dve.tensor_scalar(ssq[:, :], ssq[:, :], 1.0 / D, EPS, ALU.mult, ALU.add).then_inc(S("ssq_ready"), 1)
            for k in range(KT):
                dve.wait_ge(S("x_turned"), k + 1)
                dve.tensor_copy(xr_t[:, k, :], bank(4 + k % 4)).then_inc(S("xr_ready"), 1)
            dve.wait_ge(S("mod_cols_done"), 1)
            dve.wait_ge(S("cols_ready"), 3)
            dve.tensor_tensor(mod_t[:, :, :], bank(2)[:, 0:64].rearrange("p (k s) -> p k s", s=2),
                              cols[:, 80:112].rearrange("p (k o) -> p k o", o=1).broadcast_to([P, 32, 2]), ALU.add)\
                .then_inc(S("mod_ready"), 1)
            dve.wait_ge(S("mod_ready"), 1)
            for e in range(2):
                dve.scalar_tensor_tensor(out=scale1[:, e, :], in0=mod_t[:, KT:2 * KT, e], scalar=1.0,
                                         in1=cols[:, 2 * KT:3 * KT], op0=ALU.add, op1=ALU.mult).then_inc(S("scale1_ready"), 1)
            dve.wait_ge(S("scale1_ready"), 2)
            dve.wait_ge(S("xr_ready"), KT)
            for j in range(8):
                for k in (2 * j, 2 * j + 1):
                    for e in range(2):
                        t = xr_t[:, k, e * L:(e + 1) * L]
                        dve.tensor_scalar(t, t, scale1[:, e, k:k + 1], mod_t[:, k, e:e + 1], ALU.mult, ALU.add)\
                            .then_inc(S("h1_ready"), 1)
                    for e, (lo, hi) in enumerate(((h_lo, h_hi), (hc_lo, hc_hi))):
                        dve.wait_ge(S("h1_hi"), 2 * k + e + 1)
                        dve.tensor_tensor(lo[:, k, :], xr_t[:, k, e * L:(e + 1) * L], hi[:, k, :].bitcast(F32),
                                          ALU.subtract).then_inc(S("h1_lo"), 1)
                split(0, j)
            dve.wait_ge(S("h1_lo"), 2 * KT)
            for j in range(8):
                add_chunk(0, j, 0, j)
                split(8, j)
            with dve.Fori(0, 2) as i:
                for u in range(2):
                    for j in range(8):
                        n = 8 + 8 * u + j
                        add_chunk(i, n, *chunk_of(n))
                        split(i * 16 + (16 + 8 * u), j)
            for j in range(8):
                add_chunk(0, 40 + j, *chunk_of(40 + j))
                split(48, j)
            dve.wait_ge(S("ga_hi_ready"), 1)
            dve.tensor_tensor(ga_lo[:, :, :], ga_w[:, :, :], ga_hi[:, :, :].bitcast(F32), ALU.subtract)\
                .then_inc(S("ga_lo_ready"), 1)

            def at_pre(p):
                if p in (5, 7):
                    d = (p - 5) // 2
                    t = la[:, d, :, :].rearrange("p m n -> p (m n)")
                    dve.wait_ge(S("la_step"), 3 * d + 3)
                    dve.scalar_tensor_tensor(out=t, in0=bank(4, 4), scalar=0.0, in1=t, op0=ALU.min, op1=ALU.subtract)\
                        .then_inc(S("la_ready"), 1)
                if p in (13, 14):
                    d = p - 13
                    dve.wait_ge(S("kw_exp"), d + 1)
                    dve.wait_ge(S("gkc_landed"), 16)
                    dve.tensor_tensor(kw[:, d, :, :], kw[:, d, :, :], gkc[:, :, :], ALU.mult).then_inc(S("kw_ready"), 1)
                if p == 17:
                    dve.wait_ge(S("mod2_done"), 1)
                    m = bank(4)[:, 0:64]
                    dve.tensor_tensor(mod2[:, :, :], m[:, KT:3 * KT].rearrange("p (a k) -> p a k", a=2),
                                      cols2[:, KT:3 * KT].rearrange("p (a k) -> p a k", a=2), ALU.add)\
                        .then_inc(S("mod2_step"), 1)
                    for d, (a, b) in enumerate(((0, 64), (48, 80))):
                        dve.tensor_tensor(gw_cols[:, d, :], m[:, a:a + KT], cols2[:, a:a + KT], ALU.add)\
                            .then_inc(S("mod2_step"), 1)
                    dve.wait_ge(S("mod2_step"), 3)
                    dve.scalar_tensor_tensor(out=mod2[:, 1, :], in0=mod2[:, 1, :], scalar=1.0, in1=cols[:, 3 * KT:4 * KT],
                                             op0=ALU.add, op1=ALU.mult).then_inc(S("mod2_step"), 1)
                    dve.tensor_tensor(gw_cols[:, :, :], gw_cols[:, :, :],
                                      cols2[:, 64:96].rearrange("p (a k) -> p a k", a=2), ALU.mult)\
                        .then_inc(S("mod2_step"), 1)

            for t in range(3):
                for j in range(8):
                    at_pre(8 * t + j)
                    n = 48 + 8 * t + j
                    if n < 4 * KT:
                        add_chunk(0, n, *chunk_of(n))
                    split(S_LAT + 8 * t, j)
            with dve.Fori(0, 2) as i:
                for j in range(16):
                    split(i * 16 + (S_LAT + 24), j)

            def exponents(i, first):
                for e in range(4):
                    h = LEVELS[first + e]
                    n = L // (2 * h)

                    def view(d, a):
                        return cum[:, d, bass.ds(i, 1), a:a + L].rearrange("p o (b u e) -> p (o b) u e", u=2, e=h)

                    def mid(d):
                        return view(d, 0)[:, :, 1, 0:1].broadcast_to([P, n, h])

                    q = g_arg[:, 0, e, :].rearrange("p (b u e) -> p b u e", u=2, e=h)
                    k = g_arg[:, 1, e, :].rearrange("p (b u e) -> p b u e", u=2, e=h)
                    dve.tensor_tensor(q[:, :, 1, :], view(0, 1)[:, :, 1, :], mid(0), ALU.subtract)
                    dve.tensor_tensor(q[:, :, 0, :], mid(1), view(1, 0)[:, :, 0, :], ALU.subtract)
                    dve.tensor_tensor(k[:, :, 0, :], mid(0), view(0, 1)[:, :, 0, :], ALU.subtract)
                    last = dve.tensor_tensor(k[:, :, 1, :], view(1, 0)[:, :, 1, :], mid(1), ALU.subtract)
                last.then_inc(S("g_arg_ready"), 1)

            def hold(n):
                dve.memset(spare[:, n:n + 1], 0.0)

            def weigh(i, r):
                dve.wait_ge(S("g_exp_ready"), i * 2 + (r + 1))
                for a in range(2):
                    last = dve.tensor_tensor(g_arg[:, a, :, :], g_arg[:, a, :, :],
                                             g_qkt[:, a:a + 1, :].broadcast_to([P, 4, L]), ALU.mult)
                last.then_inc(S("g_qk_ready"), 1)

            def pick(i, r, n):
                dve.wait_ge(S("g_levels_done"), i * 2 + (r + 1))
                if r == 1:
                    dve.wait_ge(S("g_cross_ready"), i + 1)
                for e in range(n):
                    if r == 1 or e > 0:
                        dve.wait_ge(S("g_picked"), i * 7 + (4 * r + e))
                    else:
                        dve.wait_ge(S("g_diag_ready"), i + 1)
                    hold(4 * r + e)
                    src = bank(6, 2)[:, e * L:(e + 1) * L].rearrange("p (a n) -> p a n", a=2)
                    dve.copy_predicated(g_a[:, 0:2, :],
                                        mask[:, 4 * r + e:4 * r + e + 1, :].broadcast_to([P, 2, P]), src)\
                        .then_inc(S("g_picked"), 1)

            with dve.Fori(0, RH) as i:
                for p in range(16):
                    if p == 4:
                        dve.wait_ge(S("g_qk_landed"), i * 32 + 32)
                        exponents(i, 0)
                        dve.tensor_tensor(g_st[:, 1:2, :], cum[:, 1, bass.ds(i, 1), L:L + 1].broadcast_to([P, 1, L]),
                                          cum[:, 1, bass.ds(i, 1), 0:L], ALU.subtract).then_inc(S("g_st_arg"), 1)
                    if p == 5:
                        dve.wait_ge(S("g_qkt_ready"), i * 2 + 2)
                        weigh(i, 0)
                        dve.wait_ge(S("g_st_exp"), i * 2 + 2)
                        dve.tensor_tensor(g_st[:, :, :], g_st[:, :, :], g_qkt[:, 0:1, :].broadcast_to([P, 2, L]), ALU.mult)\
                            .then_inc(S("g_st_ready"), 1)
                    if p == 6:
                        dve.wait_ge(S("g_diag_done"), i + 1)
                        dve.tensor_tensor(g_a[:, 0:2, :], bank(7)[:, 0:L].rearrange("p (a n) -> p a n", a=2),
                                          ident[:, :].rearrange("p (o n) -> p o n", o=1).broadcast_to([P, 2, P]),
                                          ALU.mult).then_inc(S("g_diag_ready"), 1)
                    if p == 7:
                        pick(i, 0, 4)
                        exponents(i, 4)
                    if p == 8:
                        weigh(i, 1)
                    if p == 9:
                        pick(i, 1, 3)
                    if p == 10:
                        dve.wait_ge(S("g_o_done"), i + 1)
                        for m in range(MT):
                            dve.bn_stats(stats[:, 1, m, :], bank(6)[:, m * GDV:(m + 1) * GDV]).then_inc(S("g_stat"), 1)
                        dve.wait_ge(S("g_stat"), i * 5 + 2)
                        hold(7)
                        for m in range(MT):
                            dve.bn_aggr(mv[:, 1, m, :], stats[:, 1, m, :]).then_inc(S("g_stat"), 1)
                        dve.wait_ge(S("g_stat"), i * 5 + 4)
                        dve.tensor_tensor(mv[:, 1, :, 0:1], mv[:, 1, :, 0:1], mv[:, 1, :, 0:1], ALU.mult)\
                            .then_inc(S("g_stat"), 1)
                        dve.wait_ge(S("g_stat"), i * 5 + 5)
                        dve.scalar_tensor_tensor(out=mv[:, 1, :, 0:1], in0=mv[:, 1, :, 0:1], scalar=EPS,
                                                 in1=mv[:, 1, :, 1:2], op0=ALU.add, op1=ALU.add)\
                            .then_inc(S("g_ms_ready"), 1)
                    if p == 11:
                        dve.wait_ge(S("g_rstd_ready"), i + 1)
                        dve.wait_ge(S("g_silu"), i + 1)
                        for m in range(MT):
                            last = dve.scalar_tensor_tensor(out=g_g[:, m, :], in0=bank(6)[:, m * GDV:(m + 1) * GDV],
                                                            scalar=hr[:, 1, m, :], in1=g_g[:, m, :],
                                                            op0=ALU.mult, op1=ALU.mult)
                        last.then_inc(S("g_on_ready"), 1)
                    if p == 12:
                        dve.wait_ge(S("r_scores_done"), i + 1)
                        dve.tensor_tensor(r_a[:, :, :], bank(4, 2).rearrange("p (a n) -> p a n", a=4),
                                          dmat[:, bass.ds(i, 1), :, :].rearrange("p o a n -> p (o a) n"), ALU.mult)\
                            .then_inc(S("r_a_ready"), 1)
                        dve.wait_ge(S("g_on_turned"), i + 1)
                        dve.tensor_tensor(o_t[:, 1, bass.ds(i * 2, 2), :], bank(7).rearrange("p (a n) -> p a n", a=2),
                                          cols[:, bass.ds(i * 2 + 72, 2)].rearrange("p (a o) -> p a o", o=1)
                                          .broadcast_to([P, 2, L]), ALU.mult).then_inc(S("gla_head_done"), 1)
                    if p == 13:
                        dve.wait_ge(S("r_o_done"), i + 1)
                        for m in range(MT):
                            dve.bn_stats(stats[:, 0, m, :], bank(4)[:, m * RDK:(m + 1) * RDK]).then_inc(S("r_stat"), 1)
                        dve.wait_ge(S("r_stat"), i * 4 + 2)
                        hold(8)
                        for m in range(MT):
                            dve.bn_aggr(mv[:, 0, m, :], stats[:, 0, m, :]).then_inc(S("r_stat"), 1)
                        dve.wait_ge(S("r_stat"), i * 4 + 4)
                        dve.tensor_scalar(mv[:, 0, :, 1:2], mv[:, 0, :, 1:2], EPS, None, ALU.add)\
                            .then_inc(S("r_var_ready"), 1)
                    if p == 14:
                        dve.wait_ge(S("r_silu"), i + 1)
                        for m in range(MT):
                            dve.scalar_tensor_tensor(out=r_g[:, m, :], in0=bank(4)[:, m * RDK:(m + 1) * RDK],
                                                     scalar=mv[:, 0, m, 0:1], in1=r_g[:, m, :],
                                                     op0=ALU.subtract, op1=ALU.mult).then_inc(S("r_centred"), 1)
                        dve.wait_ge(S("r_rstd_ready"), i + 1)
                        dve.wait_ge(S("r_centred"), i * 2 + 2)
                        for m in range(MT):
                            last = dve.tensor_scalar(r_g[:, m, :], r_g[:, m, :], hr[:, 0, m, :], None, ALU.mult)
                        last.then_inc(S("r_on_ready"), 1)
                    if p == 15:
                        dve.wait_ge(S("r_on_turned"), i + 1)
                        dve.tensor_tensor(o_t[:, 0, bass.ds(i * 2, 2), :], bank(5).rearrange("p (a n) -> p a n", a=2),
                                          cols[:, bass.ds(i * 2 + 64, 2)].rearrange("p (a o) -> p a o", o=1)
                                          .broadcast_to([P, 2, L]), ALU.mult).then_inc(S("ret_head_done"), 1)
                    split(i * 16 + (S_LAT + 8 * 7), p)

            for g in range(2):
                dve.wait_ge(S("o_hi_ready"), g + 1)
                dve.tensor_tensor(o_lo[:, g, :, :], o_t[:, g, :, :], o_hi[:, g, :, :].bitcast(F32), ALU.subtract)\
                    .then_inc(S("o_lo_ready"), 1)

            def merge(j, n):
                if j in (0, 4):
                    g = j // 4
                    dve.wait_ge(w_used, n * 8 + (S_UP + 4 + 4 * g))
                    dve.wait_ge(S(f"gate_ready{g}"), n + 1)
                    dve.tensor_tensor(up_t[:, g, :, :], bank(2 - 2 * g, 2).rearrange("p (m n) -> p m n", m=MT),
                                      gate_s[:, g, :, :], ALU.mult).then_inc(S(f"gate_used{g}"), 1)
                if j == 4:
                    dve.wait_ge(S("gate_used0"), n + 1)
                    dve.wait_ge(S("gate_used1"), n + 1)
                    dve.tensor_tensor(mg[:, :, :], up_t[:, 0, :, :], up_t[:, 1, :, :], ALU.add).then_inc(S("mg_ready"), 1)
                if j == 6:
                    hh = bass.ds(n * 4, 4)
                    dve.wait_ge(S("turned_hi"), n + 1)
                    dve.tensor_tensor(h_lo[:, hh, :], bank(4, 2).rearrange("p (q n) -> p q n", q=4),
                                      h_hi[:, hh, :].bitcast(F32), ALU.subtract).then_inc(S("turned_lo"), 1)

            for j in range(8):
                split(S_UP, j)
            with dve.Fori(0, OUT_BLOCKS - 1) as i:
                for j in range(8):
                    merge(j, i)
                    split(i * 8 + (S_UP + 8), j)
            for n in range(OUT_BLOCKS):
                for j in range(8):
                    if n == 0:
                        merge(j, OUT_BLOCKS - 1)
                    split(S_OUT + 8 * n, j)
            for j in range(4):
                split(S_FFN, j)

            def mean_squares(r):
                dve.wait_ge(S("y_square"), 2 * OUT_BLOCKS * r)
                dve.tensor_reduce(ssq[:, 0:MT], ssy[:, :, :], AX_X, ALU.add).then_inc(S("ssy_ready"), 1)
                dve.wait_ge(S("ssy_ready"), 2 * r - 1)
                dve.tensor_scalar(ssq[:, 0:MT], ssq[:, 0:MT], 1.0 / D, EPS, ALU.mult, ALU.add).then_inc(S("ssy_ready"), 1)

            mean_squares(1)
            dve.wait_ge(S("rstd_ready"), 2)
            dve.wait_ge(S("res_landed"), 32)
            for m in range(MT):
                dve.scalar_tensor_tensor(out=y[:, m, :], in0=y[:, m, :], scalar=rstd[:, m:m + 1], in1=g1w[:, :],
                                         op0=ALU.mult, op1=ALU.mult).then_inc(S("y_scaled"), 1)
                dve.wait_ge(S("y_scaled"), m + 1)
                dve.tensor_tensor(hs[:, m, :], hs[:, m, :], y[:, m, :], ALU.add).then_inc(S("hs_ready"), 1)
            dve.wait_ge(S("square"), 4 + MT)
            dve.tensor_scalar(ssq[:, 2:4], ssq[:, 2:4], 1.0 / D, EPS, ALU.mult, ALU.add).then_inc(S("ssh_ready"), 1)

            def hidden(j, n):
                if j == 4:
                    dve.wait_ge(w_used, n * 16 + (S_FFN + 16))
                    dve.wait_ge(S("silu_ready"), n + 1)
                    dve.tensor_tensor(hid_n[:, :, :], bank(0, 2).rearrange("p (m n) -> p m n", m=MT), sg[:, :, :], ALU.mult)\
                        .then_inc(S("hid_n_ready"), 1)
                if j == 6:
                    hh = bass.ds(n * 4, 4)
                    dve.wait_ge(S("turned_hi"), n + (OUT_BLOCKS + 1))
                    dve.tensor_tensor(hid_lo[:, hh, :], bank(4, 2).rearrange("p (q n) -> p q n", q=4),
                                      hid_hi[:, hh, :].bitcast(F32), ALU.subtract).then_inc(S("turned_lo"), 1)

            for j in range(16):
                if j < 8:
                    dve.wait_ge(S("h2_hi_ready"), j + 1)
                    dve.tensor_tensor(h_lo[:, 2 * j:2 * j + 2, :], h2f[:, j % 2, :, :],
                                      h_hi[:, 2 * j:2 * j + 2, :].bitcast(F32), ALU.subtract).then_inc(S("h2_lo_ready"), 1)
                if j >= 4:
                    split(S_FFN, j)
            with dve.Fori(0, FF_BLOCKS - 1) as i:
                for j in range(16):
                    hidden(j, i)
                    split(i * 16 + (S_FFN + 16), j)
            for n in range(OUT_BLOCKS):
                for j in range(DOWN_SLOTS):
                    if n == 0:
                        hidden(j, FF_BLOCKS - 1)
                    split(S_DOWN + n * DOWN_SLOTS, j)
            mean_squares(2)
            dve.wait_ge(S("rstd_ready"), 4)
            dve.wait_ge(S("end_landed"), 32)
            for m in range(MT):
                for n in range(OUT_BLOCKS):
                    t = y2[:, m, n * N:(n + 1) * N]
                    dve.scalar_tensor_tensor(out=t, in0=t, scalar=rstd[:, m:m + 1], in1=g2w[:, n * N:(n + 1) * N],
                                             op0=ALU.mult, op1=ALU.mult).then_inc(S("y_scaled"), 1)
                    dve.wait_ge(S("y_scaled"), MT + OUT_BLOCKS * m + n + 1)
                    dve.tensor_tensor(t, t, hs2[:, m, n * N:(n + 1) * N], ALU.add).then_inc(S("final_ready"), 1)

        @block.tensor
        def _(pe):
            def products(s, j, k, last_k, tiles, first_bank):
                if isinstance(s, int):
                    s, j = 0, s + j
                q = j % SPLIT
                pe.wait_ge(w_low, s + (j + 1))
                for e in range(2):
                    for n, (hi, lo, m) in enumerate(tiles):
                        o = bank(first_bank + n)
                        kk, c = k + e, slice(m * P, (m + 1) * P)
                        pe.matmul(o, hi[:, kk, c], w_hi[:, q, e, :], start=kk == 0, stop=False)
                        pe.matmul(o, hi[:, kk, c], w_lo[:, q, e, :], start=False, stop=False)
                        last = pe.matmul(o, lo[:, kk, c], w_hi[:, q, e, :], start=False, stop=kk == last_k)
                last.then_inc(w_used, 1)
                return last

            LAT = [(h_hi, h_lo, 0), (h_hi, h_lo, 1)]
            CTX = LAT + [(hc_hi, hc_lo, 0), (hc_hi, hc_lo, 1)]

            pe.wait_ge(S("rows_landed"), 16 * 11)
            pe.transpose(bank(7)[:, 0:112], rows[0:112, :], ident[0:112, 0:112])
            pe.transpose(bank(7)[:, 128:224], rows2[:, :], ident[0:96, 0:96]).then_inc(S("cols_turned"), 1)
            pe.wait_ge(S("cols_ready"), 1)
            c2 = csil[:, :].rearrange("p (s k) -> p s k", s=2)
            for n in range(MOD_BLOCKS):
                if n >= 2:
                    pe.wait_ge(S("mod_row_ready"), n - 1)
                for j in range(8):
                    pe.wait_ge(landed[j], 16 * (n + 1))
                    for e in range(2):
                        k = 2 * j + e
                        last = pe.matmul(bank(n % 2)[0:2, :], c2[:, :, k], raw[:, j, e, :], start=k == 0, stop=k == KT - 1)
                    last.then_inc(mod_used, 1)
                if 1 <= n <= 4:
                    pe.wait_ge(S("x_scaled"), 4)
                    pe.wait_ge(S("cols_ready"), 3)
                    for k in range(4 * (n - 1), 4 * n):
                        if k >= 4:
                            pe.wait_ge(S("xr_ready"), k - 3)
                        for m in range(4):
                            last = pe.transpose(bank(4 + k % 4)[:, m * P:(m + 1) * P], xn[:, m, k * P:(k + 1) * P], ident[:, :])
                        last.then_inc(S("x_turned"), 1)
            pe.wait_ge(S("mod_row_ready"), MOD_BLOCKS)
            for r in range(32):
                last = pe.transpose(bank(2)[:, 2 * r:2 * r + 2], mod_row[:, r // 4, (r % 4) * P:(r % 4 + 1) * P], ident[0:2, 0:2])
            last.then_inc(S("mod_cols_done"), 1)
            pe.wait_ge(S("mod_ready"), 1)

            def ctx_block(s, b, group):
                if not isinstance(b, int) or b >= 2:
                    pe.wait_ge(staged[3], b + (-1))
                for j in range(8):
                    if isinstance(b, int) and b == 0:
                        pe.wait_ge(S("h1_lo"), 4 * j + 4)
                    products(s, j, 2 * j, KT - 1, CTX, 4 * group)

            ctx_block(0, 0, 0)
            ctx_block(8, 1, 1)
            with pe.Fori(0, 2) as i:
                for u in range(2):
                    ctx_block(i * 16 + (16 + 8 * u), i * 2 + (2 + u), u)
            ctx_block(48, 6, 0)
            pe.wait_ge(staged[3], 6)
            pe.wait_ge(S("ga_lo_ready"), 1)
            for n, (hi, lo, m) in enumerate(CTX):
                o = bank(4)[:, n * 2 * LOW:(n + 1) * 2 * LOW]
                for k in range(KT):
                    c = slice(m * P, (m + 1) * P)
                    pe.matmul(o, hi[:, k, c], ga_hi[:, k, :], start=k == 0, stop=False)
                    pe.matmul(o, hi[:, k, c], ga_lo[:, k, :], start=False, stop=False)
                    last = pe.matmul(o, lo[:, k, c], ga_hi[:, k, :], start=False, stop=k == KT - 1)
            last.then_inc(S("ga_done"), 1)

            def at_pre(p):
                if p == 4:
                    pe.wait_ge(S("ga_n_ready"), 1)
                    for m in range(4):
                        last = pe.transpose(bank(4)[0:2 * LOW, m * P:(m + 1) * P], ga_n[:, m, :], ident[:, :])
                    last.then_inc(S("ga_turned"), 1)
                if p in (5, 7):
                    d = (p - 5) // 2
                    pe.wait_ge(S("al_ready"), 1)
                    pe.wait_ge(S("a_up_landed"), 48)
                    if d == 1:
                        pe.wait_ge(S("la_ready"), 1)
                    for m in range(4):
                        last = pe.matmul(bank(4 + m), al_t[:, m * P:(m + 1) * P], a_up[:, d, :], start=True, stop=True)
                    last.then_inc(S("z_done"), 1)
                if p in (9, 10):
                    d = p - 9
                    pe.wait_ge(S("la_ready"), 2)
                    if d == 1:
                        pe.wait_ge(S("cum_ready"), 1)
                    for h in range(GH):
                        for m in range(MT):
                            last = pe.matmul(bank(4 + h)[:, 0:L + 1], la[:, d, m, h * GDK:(h + 1) * GDK],
                                             before[:, m, :], start=m == 0, stop=m == MT - 1)
                    last.then_inc(S("sums_done"), 1)
                if p in (12, 13):
                    d = p - 12
                    pe.wait_ge(S("cum_ready"), 2)
                    for q in range(MT):
                        for m in range(MT):
                            t = (after if d == 0 else before)[:, m, q * P:(q + 1) * P]
                            last = pe.matmul(bank(4 + 2 * d + q), t, la[:, d, 2 + m, :], start=m == 0, stop=m == MT - 1)
                    last.then_inc(S("ctx_sums_done"), 1)
                if p == 16:
                    pe.wait_ge(S("wm_used"), 4 * KT)
                    pe.wait_ge(S("kw_exp"), 2)
                    for r in range(64):
                        g, k = divmod(r, KT)
                        last = pe.matmul(bank(4)[:, r:r + 1], acc[:, g, k * P:(k + 1) * P], ones[:, :], start=True, stop=True)
                    last.then_inc(S("mod2_done"), 1)
                if p == 18:
                    pe.wait_ge(S("mod2_step"), 5)
                    pe.transpose(bank(5)[0:2 * KT, 0:P], gw_cols[:, :, :].rearrange("p a k -> p (a k)"), ident[:, :])\
                        .then_inc(S("gw_turned"), 1)

            def lat_block(s, i, t, at):
                if isinstance(i, int) and t < 2:
                    pe.wait_ge(staged[3], CTX_BLOCKS)
                else:
                    pe.wait_ge(staged[2 * (t % 2) + 1], i + (CTX_BLOCKS + t // 2))
                for j in range(8):
                    products(s, j, 2 * j, KT - 1, LAT, 2 * (t % 2))
                    at(j)

            pe.wait_ge(S("ones_ready"), 1)
            pe.wait_ge(S("consts_landed"), 16 * 5)
            for t in range(3):
                lat_block(S_LAT + 8 * t, 0, t, lambda j: at_pre(8 * t + j + 4))
            with pe.Fori(0, 2) as i:
                for u in range(2):
                    lat_block(i * 16 + (S_LAT + 24 + 8 * u), i, 3 + u, lambda j: None)

            def at_head(i, p):
                if p == 5:
                    pe.wait_ge(S("g_qk_landed"), i * 32 + 32)
                    for a, t in enumerate((g_q, g_k)):
                        for m in range(MT):
                            last = pe.transpose(bank(6)[:, a * L + m * P:a * L + (m + 1) * P], t[:, m, :], ident[:, :])
                    last.then_inc(S("g_qk_turned"), 1)
                if p == 6:
                    pe.wait_ge(S("g_qkt_ready"), i * 2 + 2)
                    for m in range(MT):
                        last = pe.matmul(bank(7)[:, m * P:(m + 1) * P], g_qkt[:, 1, m * P:(m + 1) * P],
                                         g_qkt[:, 0, m * P:(m + 1) * P], start=True, stop=True)
                    last.then_inc(S("g_diag_done"), 1)
                    pe.wait_ge(S("g_v_landed"), i * 64 + 64)
                    for d in range(2):
                        for m in range(MT):
                            last = pe.matmul(bank(6)[:, d * GDV:(d + 1) * GDV], g_kw[:, d, m, :], g_v[:, m, :],
                                             start=m == 0, stop=m == MT - 1)
                    last.then_inc(S("g_state_done"), 1)
                    pe.wait_ge(S("r_kc_landed"), i * 16 + 16)
                    for f in range(2):
                        for m in range(MT):
                            last = pe.transpose(bank(4)[:, f * L + m * P:f * L + (m + 1) * P],
                                                r_kc[:, m, f * P:(f + 1) * P], ident[:, :])
                    last.then_inc(S("r_kc_turned"), 1)
                if p in (7, 9):
                    r = (p - 7) // 2
                    pe.wait_ge(S("g_qk_ready"), i * 2 + (r + 1))
                    if r == 0:
                        pe.wait_ge(S("g_s_ready"), i + 1)
                        pe.wait_ge(S("g_diag_ready"), i + 1)
                    else:
                        pe.wait_ge(S("g_picked"), i * 7 + 4)
                    for e in range(4):
                        for m in range(MT):
                            key = m
                            qry = m if 4 * r + e < 7 else 1 - m
                            last = pe.matmul(bank(6, 2)[:, e * L + m * P:e * L + (m + 1) * P],
                                             g_arg[:, 1, e, key * P:(key + 1) * P], g_arg[:, 0, e, qry * P:(qry + 1) * P],
                                             start=True, stop=True)
                    last.then_inc(S("g_levels_done"), 1)
                if p == 8:
                    pe.wait_ge(S("rope_ready"), i * 4 + 4)
                    pe.wait_ge(S("r_kct_ready"), i + 1)
                    for b, t in ((5, r_q), (4, r_k)):
                        for f in range(2):
                            for m in range(MT):
                                last = pe.transpose(bank(b)[:, f * L + m * P:f * L + (m + 1) * P],
                                                    t[:, m, f * P:(f + 1) * P], ident[:, :])
                    last.then_inc(S("r_qk_turned"), 1)
                if p == 10:
                    pe.wait_ge(S("g_picked"), i * 7 + 7)
                    pe.wait_ge(S("g_cross_ready"), i + 1)
                    pe.wait_ge(S("g_st_ready"), i + 1)
                    for m in range(MT):
                        o, c = bank(6)[:, m * GDV:(m + 1) * GDV], slice(m * P, (m + 1) * P)
                        pe.matmul(o, g_a[:, m, :], g_v[:, 2 + m, :], start=True, stop=False)
                        pe.matmul(o, g_a[:, 3 - m, :], g_v[:, 3 - m, :], start=False, stop=False)
                        pe.matmul(o, g_st[:, 0, c], g_s[:, 0, :], start=False, stop=False)
                        last = pe.matmul(o, g_st[:, 1, c], g_s[:, 1, :], start=False, stop=True)
                    last.then_inc(S("g_o_done"), 1)
                if p == 11:
                    pe.wait_ge(S("r_qkt_ready"), i * 2 + 2)
                    for a in range(4):
                        for f in range(2):
                            last = pe.matmul(bank(4, 2)[:, a * L:(a + 1) * L],
                                             r_kt[:, 2 * (a // 2) + f, (a % 2) * P:(a % 2 + 1) * P], r_qt[:, f, :],
                                             start=f == 0, stop=f == 1)
                    last.then_inc(S("r_scores_done"), 1)
                if p == 12:
                    pe.wait_ge(S("g_on_ready"), i + 1)
                    for f in range(2):
                        for m in range(MT):
                            last = pe.transpose(bank(7)[:, f * L + m * P:f * L + (m + 1) * P],
                                                g_g[:, m, f * P:(f + 1) * P], ident[:, :])
                    last.then_inc(S("g_on_turned"), 1)
                if p == 13:
                    pe.wait_ge(S("r_a_ready"), i + 1)
                    pe.wait_ge(S("r_v_landed"), i * 32 + 32)
                    for m in range(MT):
                        for a in range(4):
                            last = pe.matmul(bank(4)[:, m * RDK:(m + 1) * RDK], r_a[:, a, m * P:(m + 1) * P],
                                             r_v[:, a, :], start=a == 0, stop=a == 3)
                    last.then_inc(S("r_o_done"), 1)
                if p == 15:
                    pe.wait_ge(S("r_on_ready"), i + 1)
                    for f in range(2):
                        for m in range(MT):
                            last = pe.transpose(bank(5)[:, f * L + m * P:f * L + (m + 1) * P],
                                                r_g[:, m, f * P:(f + 1) * P], ident[:, :])
                    last.then_inc(S("r_on_turned"), 1)

            with pe.Fori(0, RH) as i:
                for u in range(2):
                    lat_block(i * 16 + (S_LAT + 56 + 8 * u), i, 7 + u, lambda j: at_head(i, 8 * u + j + 4))

            def turn_columns(src, ready, freed, n):
                pe.wait_ge(S(ready), n + 1)
                if freed is not None:
                    pe.wait_ge(S(freed), n)
                for q in range(4):
                    for m in range(MT):
                        last = pe.transpose(bank(4, 2)[:, q * L + m * P:q * L + (m + 1) * P],
                                            src[:, m, q * P:(q + 1) * P], ident[:, :])
                last.then_inc(S("turned"), 1)

            def up_block(s, n, prev, first_prev):
                for g in range(2):
                    pe.wait_ge(S("o_lo_ready"), g + 1)
                    if prev is None:
                        pe.wait_ge(staged[3 - 2 * g], 14 + g)
                    else:
                        pe.wait_ge(S(f"gate_used{g}"), n)
                    for j in range(4):
                        tiles = [(o_hi[:, g], o_lo[:, g], 0), (o_hi[:, g], o_lo[:, g], 1)]
                        products(s, 4 * g + j, 2 * j, 7, tiles, 2 - 2 * g)
                        if prev is not None and g == 0 and j == 2:
                            turn_columns(mg, "mg_ready", None if first_prev else "turned_lo", prev)
            up_block(S_UP, 0, None, False)
            with pe.Fori(0, OUT_BLOCKS - 1) as i:
                up_block(i * 8 + (S_UP + 8), i + 1, i, True)

            for n in range(OUT_BLOCKS):
                if n < 2:
                    pe.wait_ge(S(f"gate_used{n}"), OUT_BLOCKS)
                else:
                    pe.wait_ge(S("y_square"), 2 * (n - 1))
                for j in range(8):
                    if n == 0 and j in (0, 6):
                        pe.wait_ge(S("turned_lo"), 3 if j == 0 else 4)
                    products(S_OUT + 8 * n, j, 2 * j, KT - 1, LAT, 2 * (1 - n % 2))
                    if n == 0 and j == 2:
                        turn_columns(mg, "mg_ready", None, OUT_BLOCKS - 1)

            for j in range(8):
                if j == 0:
                    pe.wait_ge(S("h2n_ready"), MT)
                if j >= 4:
                    pe.wait_ge(S("h2_hi_ready"), j - 3)
                for e in range(2):
                    for m in range(MT):
                        last = pe.transpose(bank(4 + j % 4)[:, e * L + m * P:e * L + (m + 1) * P],
                                            h2n[:, m, (2 * j + e) * P:(2 * j + e + 1) * P], ident[:, :])
                last.then_inc(S("h2_turned"), 1)

            def ffn_block(s, n, prev):
                for g in range(2):
                    if prev is not None:
                        pe.wait_ge(S("silu_ready" if g == 0 else "hid_n_ready"), n)
                    else:
                        pe.wait_ge(S("y_square"), 2 * OUT_BLOCKS)
                    for j in range(8):
                        if prev is None and g == 0:
                            pe.wait_ge(S("h2_lo_ready"), j + 1)
                        products(s, 8 * g + j, 2 * j, KT - 1, LAT, 2 - 2 * g)
                        if prev is not None and g == 0 and j == 2:
                            turn_columns(hid_n, "hid_n_ready", None, prev)
            ffn_block(S_FFN, 0, None)
            with pe.Fori(0, FF_BLOCKS - 1) as i:
                ffn_block(i * 16 + (S_FFN + 16), i + 1, i)

            for n in range(OUT_BLOCKS):
                if n == 0:
                    pe.wait_ge(S("silu_ready"), FF_BLOCKS)
                elif n == 1:
                    pe.wait_ge(S("hid_n_ready"), FF_BLOCKS)
                else:
                    pe.wait_ge(S("y_square"), 2 * (OUT_BLOCKS + n - 1))
                HID = [(hid_hi, hid_lo, 0), (hid_hi, hid_lo, 1)]
                for j in range(DOWN_SLOTS):
                    if n == 0 and j in (0, 20):
                        pe.wait_ge(S("turned_lo"), OUT_BLOCKS + FF_BLOCKS - (j == 0))
                    products(S_DOWN + n * DOWN_SLOTS, j, 2 * j, D_FF // P - 1, HID, 2 * (1 - n % 2))
                    if n == 0 and j == 2:
                        turn_columns(hid_n, "hid_n_ready", None, FF_BLOCKS - 1)


WIDE = ["w_mod", "b_mod", "norm_mix_pre", "norm_mix_post", "norm_ffn_pre", "norm_ffn_post", "w_in", "ret_decay",
        "gla_a_up", "gla_a_bias", "ret_gn", "gla_gn", "w_up_ret", "w_up_gla", "w_out", "ffn_w_gate", "ffn_w_up",
        "ffn_w_down"]


def kernel(**inputs):
    import concourse.bacc as bacc
    from concourse.bass_utils import run_bass_kernel_spmd as run

    nc = bacc.Bacc("TRN2", target_bir_lowering=False, num_devices=1)
    arrays = {"x": np.asarray(inputs["x"])[0], "c": np.asarray(inputs["c"])[0],
              "ctx_in": np.asarray(inputs["ctx"])[0], "c_ctx": np.asarray(inputs["c_ctx"])}
    arrays.update({n: np.asarray(inputs[n])[0] for n in WIDE})
    arrays.update(constants())
    arrays = {n: np.ascontiguousarray(a) for n, a in arrays.items()}
    args = {n: nc.dram_tensor(f"in_{n}", a.shape, mybir.dt.from_np(a.dtype), kind="ExternalInput").ap()
            for n, a in arrays.items()}
    out = nc.dram_tensor("result", (L, D), F32, kind="ExternalOutput").ap()
    build(nc, **args, out=out)
    r = run(nc, [{f"in_{n}": a for n, a in arrays.items()}], core_ids=[0])
    return r.results[0]["result"][None]
```

```python
import math
from contextlib import ExitStack

import numpy as np

import concourse.bass as bass
from concourse import mybir

F32 = mybir.dt.float32
F32R = mybir.dt.float32r
U8 = mybir.dt.uint8
ALU = mybir.AluOpType
ACT = mybir.ActivationFunctionType
AX_X = mybir.AxisListType.X

P = 128
D = 2048
KT = D // P
L = 256
MT = L // P
N = 512
RH, RDK = 4, 256
GH, GDK, GDV = 4, 128, 256
LOW = 16
D_FF = ((8 * D // 3 + 255) // 256) * 256
C_RK, C_RV, C_GK, C_GV, C_GA = 0, 1024, 2048, 2560, 3584
C_RQ, C_RG, C_GQ, C_GG, C_GATE_A = 3616, 4640, 5664, 6176, 7200
D_IN = 11296
EPS = 1e-6
GATE_NORM = 16.0

CTX_BLOCKS = C_GA // N
LAT_BLOCKS = (D_IN - C_RQ) // N
FF_BLOCKS = D_FF // N
OUT_BLOCKS = D // N
RAW, SPLIT = 8, 4
MOD_BLOCKS = 8
QUARTERS = 4
LEVELS = [1, 2, 4, 8, 16, 32, 64, 128]


def constants():
    f = np.float32
    n_f = RDK // 4
    inv = (f(10000.0) ** (-np.arange(n_f, dtype=f) / f(n_f))).astype(f)
    t = np.arange(L)
    ang = np.concatenate([(t // 64).astype(f)[:, None] * inv, (t % 64).astype(f)[:, None] * inv], axis=-1)
    rope = np.stack([np.cos(ang), np.sin(ang)], axis=1).astype(f)
    rope = rope.reshape(MT, P, 2, P).transpose(1, 2, 0, 3)
    s = np.arange(L)[:, None]
    before = (s < np.arange(L + 1)[None, :]).astype(f).reshape(MT, P, L + 1).transpose(1, 0, 2)
    after = (s > np.arange(L)[None, :]).astype(f).reshape(MT, P, L).transpose(1, 0, 2)
    i = np.arange(L)[None, :]
    delta = i - s
    dist = np.stack([np.maximum(delta, 0), np.maximum(-delta, 0), i + L - s, L - i + s], axis=0).astype(f)
    dist = dist.reshape(4, MT, P, L).transpose(2, 0, 1, 3)
    a, b = np.arange(P)[:, None], np.arange(P)[None, :]
    mask = np.stack([((a // h != b // h) & (a // (2 * h) == b // (2 * h))) for h in LEVELS[:-1]], axis=1)
    take = np.array([[1, 0], [0, 1], [1, 0], [0, 1]], dtype=f)
    return {"k_ident": np.eye(P, dtype=f), "k_take": take, "k_rope": np.ascontiguousarray(rope),
            "k_before": np.ascontiguousarray(before), "k_after": np.ascontiguousarray(after),
            "k_dist": np.ascontiguousarray(dist),
            "k_mask": np.ascontiguousarray(mask.astype(f))}


def build(nc, x, c, ctx_in, c_ctx, w_mod, b_mod, norm_mix_pre, norm_mix_post, norm_ffn_pre, norm_ffn_post,
          w_in, ret_decay, gla_a_up, gla_a_bias, ret_gn, gla_gn, w_up_ret, w_up_gla, w_out,
          ffn_w_gate, ffn_w_up, ffn_w_down, k_ident, k_take, k_rope, k_before, k_after, k_dist, k_mask,
          out):
    px = nc.dram_tensor("px", (L, D_IN), F32, kind="Internal").ap()
    pc = nc.dram_tensor("pc", (L, C_GA), F32, kind="Internal").ap()
    kwd = nc.dram_tensor("kwd", (2, L, GH * GDK), F32, kind="Internal").ap()
    gwd = nc.dram_tensor("gwd", (2, D), F32, kind="Internal").ap()
    accd = nc.dram_tensor("accd", (3, P, D), F32, kind="Internal").ap()
    hsd = nc.dram_tensor("hsd", (L, D), F32, kind="Internal").ap()

    with ExitStack() as ctx:
        cursor = [(nc.sbuf_base + 31) // 32 * 32]

        def at(name, shape, dt, offset):
            return nc.alloc_sbuf_tensor_at(name, shape, dt, offset=offset)

        def keep(name, shape, dt=F32):
            size = math.prod(shape[1:]) * (4 if dt != mybir.dt.uint8 else 1)
            off = cursor[0]
            cursor[0] += (size + 31) // 32 * 32
            return at(name, shape, dt, off)

        sems = {}

        def S(name):
            if name not in sems:
                sems[name] = ctx.enter_context(nc.semaphore(name))
            return sems[name]

        raw = keep("raw", [P, RAW, 2, N])
        w_hi = keep("w_hi", [P, SPLIT, 2, N], F32R)
        w_lo = keep("w_lo", [P, SPLIT, 2, N], F32R)
        h_off = cursor[0]
        h_hi = keep("h_hi", [P, KT, L], F32R)
        h_lo = keep("h_lo", [P, KT, L], F32R)
        stage_off = cursor[0]
        stage = keep("stage", [P, 4, N])
        ident = keep("ident", [P, P])
        ones = keep("ones", [P, 1])
        rope = keep("rope", [P, 2, MT, P])
        before = keep("before", [P, MT, L + 1])
        after = keep("after", [P, MT, L])
        rows = keep("rows", [P, P])
        cols = keep("cols", [P, 112])
        cols2 = keep("cols2", [P, 96])
        gw_cols = keep("gw_cols", [P, 2, KT])
        gw_rows = keep("gw_rows", [KT, P])
        csil = keep("csil", [P, 2 * KT])
        c4 = keep("c4", [P, 4, KT], F32R)
        take = keep("take", [4, 2])
        mod_t = keep("mod_t", [P, 32, 2])
        scale1 = keep("scale1", [P, 2, KT])
        mod2 = keep("mod2", [P, 2, KT])
        lg = keep("lg", [P, 2 * RH])
        mask = keep("mask", [P, 7, P], U8)
        spare = keep("spare", [P, 16])
        ssq = keep("ssq", [P, 4])
        rstd = keep("rstd", [P, 4])
        minus_half = keep("minus_half", [P, 4])
        ssy = keep("ssy", [P, MT, OUT_BLOCKS])
        stats = keep("stats", [P, 2, MT, 6])
        mv = keep("mv", [P, 2, MT, 2])
        hr = keep("hr", [P, 2, MT, 1])
        base = cursor[0]
        K = 1024

        def reg(name, shape, kb, dt=F32):
            return at(name, shape, dt, base + kb * K)

        xn = at("xn", [P, 4, D], F32, h_off)
        xr_t = reg("xr_t", [P, KT, 4 * P], 0)
        acc = reg("acc", [P, 4, D], 0)
        hc_hi = reg("hc_hi", [P, KT, L], 32, F32R)
        hc_lo = reg("hc_lo", [P, KT, L], 48, F32R)
        mask_f = reg("mask_f", [P, 7, P], 88)
        rows2 = reg("rows2", [96, P], 92)
        junk0 = reg("junk0", [P, D], 32)
        diag0 = reg("diag0", [P, 4, P], 82)
        mod_row = reg("mod_row", [4, MOD_BLOCKS, N], 64)
        wm = reg("wm", [P, 2, D], 64)
        ga_w = reg("ga_w", [P, KT, 2 * LOW], 80)
        ga_hl = reg("ga_hl", [P, KT, 2, 2 * LOW], 82, F32R)
        la = reg("la", [P, 2, 4, GH * GDK], 32)
        cum = reg("cum", [P, 2, GH, L + 1], 48)
        dmat = reg("dmat", [P, RH, 4, L], 57)
        dist = reg("dist", [P, 4, MT, L], 73)
        kw = reg("kw", [P, 2, MT, GH * GDK], 81)
        gkc = reg("gkc", [P, MT, GH * GDK], 57)
        al_t = reg("al_t", [4 * LOW + 1, 4 * P], 90)
        a_up = reg("a_up", [4 * LOW + 1, 2, GH * GDK], 86)
        d_tmp = reg("d_tmp", [P, MT, L], 89)
        d_ctx = reg("d_ctx", [P, RH, MT, L], 81)
        r_q = reg("r_q", [P, MT, RDK], 0)
        r_k = reg("r_k", [P, MT, RDK], 2)
        r_kc = reg("r_kc", [P, MT, RDK], 4)
        r_v = reg("r_v", [P, 4, RDK], 6)
        r_g = reg("r_g", [P, MT, RDK], 10)
        r_tmp = reg("r_tmp", [P, 4, MT, P], 12)
        r_qt = reg("r_qt", [P, 2, L], 16)
        r_kt = reg("r_kt", [P, 4, L], 18)
        r_a = reg("r_a", [P, 4, L], 22)
        g_q = reg("g_q", [P, MT, GDK], 26)
        g_k = reg("g_k", [P, MT, GDK], 27)
        g_kw = reg("g_kw", [P, 2, MT, GDK], 28)
        g_v = reg("g_v", [P, 4, GDV], 30)
        g_g = reg("g_g", [P, MT, GDV], 34)
        g_qkt = reg("g_qkt", [P, 2, L], 36)
        g_arg = reg("g_arg", [P, 2, 4, L], 38)
        g_st = reg("g_st", [P, 2, L], 46)
        g_a = reg("g_a", [P, 4, P], 89)
        g_s = reg("g_s", [P, 2, GDV], 91)
        o_t = reg("o_t", [P, 2, 8, L], 73)
        o_hi = reg("o_hi", [P, 2, 8, L], 0, F32R)
        o_lo = reg("o_lo", [P, 2, 8, L], 16, F32R)
        gate_s = reg("gate_s", [P, 2, MT, N], 32)
        up_t = reg("up_t", [P, 2, MT, N], 40)
        mg = reg("mg", [P, MT, N], 48)
        y = reg("y", [P, MT, D], 52)
        acc2 = reg("acc2", [P, 3, D], 69)
        hs = reg("hs", [P, MT, D], 0)
        g1w = reg("g1w", [P, D], 16)
        junk = reg("junk", [P, D], 24)
        diag = reg("diag", [P, MT, P], 32)
        h2f = reg("h2f", [P, 2, 2, L], 48)
        hid_hi = reg("hid_hi", [P, FF_BLOCKS * 4, L], 0, F32R)
        hid_lo = reg("hid_lo", [P, FF_BLOCKS * 4, L], 44, F32R)
        hid_n = reg("hid_n", [P, MT, N], 88)
        sg = at("sg", [P, MT, N], F32, stage_off)
        g2w = at("g2w", [P, D], F32, stage_off)
        y2 = at("y2", [P, MT, D], F32, h_off)
        hs2 = at("hs2", [P, MT, D], F32, h_off + 16 * K)
        junk2 = reg("junk2", [P, N], 88)
        assert base + 93 * K <= nc.sbuf_usable_end, (base, nc.sbuf_usable_end)

        ps = ctx.enter_context(nc.psum_tensor("ps", [P, 8, N], F32))
        psf = ps[:, :, :].rearrange("p b n -> p (b n)")

        def bank(b, n=1):
            return psf[:, b * N:(b + n) * N]

        landed = [S(f"raw_landed{j}") for j in range(RAW)]
        w_high, w_low, w_used = S("w_high_ready"), S("w_low_ready"), S("w_slot_used")
        staged = [S(f"stage_written{b}") for b in range(4)]
        stored = [S(f"stage_stored{b}") for b in range(4)]

        w_in_k = w_in.rearrange("(k p) n -> p k n", p=P)
        w_mod_k = w_mod.rearrange("(k p) n -> p k n", p=P)
        w_ur_k = w_up_ret.rearrange("(k p) n -> p k n", p=P)
        w_ug_k = w_up_gla.rearrange("(k p) n -> p k n", p=P)
        w_out_k = w_out.rearrange("(k p) n -> p k n", p=P)
        w_fg_k = ffn_w_gate.rearrange("(k p) n -> p k n", p=P)
        w_fu_k = ffn_w_up.rearrange("(k p) n -> p k n", p=P)
        w_fd_k = ffn_w_down.rearrange("(k p) n -> p k n", p=P)
        px_t = px.rearrange("(m p) n -> p m n", p=P)
        pc_t = pc.rearrange("(m p) n -> p m n", p=P)

        opening = []
        for n in range(MOD_BLOCKS):
            opening += [("mod", n, j) for j in range(8)]
            opening += [("ctx", (n - 2) // 2, n % 2)] if n >= 2 else []
        opening += [("ctx", QUARTERS - 1, e) for e in range(2)]
        mod_end = [opening.index(("mod", n, 7)) for n in range(MOD_BLOCKS)]
        S_CTX = len(opening) - 8
        S_LAT = S_CTX + 8 * CTX_BLOCKS
        S_UP = S_LAT + 8 * LAT_BLOCKS
        S_OUT = S_UP + 8 * OUT_BLOCKS
        S_FFN = S_OUT + 8 * OUT_BLOCKS
        DOWN_SLOTS = D_FF // P // 2
        S_DOWN = S_FFN + 16 * FF_BLOCKS

        def chunk_of(n):
            return n // KT, n % KT

        def late_chunk(p):
            return 8 * (CTX_BLOCKS - 1) + CHUNK_AT.index(p) if p in CHUNK_AT else None

        CHUNK_AT = [0, 2, 4, 6, 9, 11, 13, 15, 17, 19, 22, 24, 26, 28, 30, 31]
        XR_AT = list(range(5, 13))
        H1_AT = [mod_end[n] + 5 for n in (1, 3, 5)]

        block = ctx.enter_context(nc.Block())

        @block.sync
        def _(sp):
            def slot(s, j, src, k, col):
                if isinstance(s, int):
                    s, j = 0, s + j
                q = j % RAW
                if not isinstance(s, int) or j >= RAW:
                    sp.wait_ge(w_low, s + (j - RAW + 1))
                sp.dma_start(raw[:, q, :, :], src[:, k:k + 2, bass.ds(col, N)]).then_inc(landed[q], 16)

            sp.dma_start(ident[:, :], k_ident).then_inc(S("rows_landed"), 16)
            r0 = 0
            for v, n in ((c, 16), (c_ctx, 16), (norm_mix_pre, 16), (norm_ffn_pre, 16), (ret_gn, 8), (gla_gn, 8),
                         (b_mod[0:2 * D], 32)):
                sp.dma_start(rows[r0:r0 + n, :], v.rearrange("(r q) -> r q", q=P)).then_inc(S("rows_landed"), 16)
                r0 += n
            for m in range(4):
                src = x if m < 2 else ctx_in
                sp.dma_start(xn[:, m, :], src[(m % 2) * P:(m % 2 + 1) * P, :]).then_inc(S(f"x_landed{m}"), 16)
            for place, (kind, n, j) in enumerate(opening):
                if kind == "mod":
                    slot(place, 0, w_mod_k, 2 * j, (n % 2) * D + (n // 2) * N)
                else:
                    slot(place, 0, w_in_k, 4 * n + 2 * j, 0)
            for j in range(8):
                slot(S_CTX + 8, j, w_in_k, 2 * j, N)
            with sp.Fori(0, (CTX_BLOCKS - 3) // 2) as i:
                for u in range(2):
                    for j in range(8):
                        slot(i * 16 + (S_CTX + 16 + 8 * u), j, w_in_k, 2 * j, i * (2 * N) + (2 + u) * N)
            for j in range(8):
                slot(S_CTX + 48, j, w_in_k, 2 * j, 6 * N)
            for t in range(3):
                for j in range(8):
                    slot(S_LAT + 8 * t, j, w_in_k, 2 * j, C_RQ + t * N)
            with sp.Fori(0, 6) as i:
                for u in range(2):
                    for j in range(8):
                        slot(i * 16 + (S_LAT + 8 * (3 + u)), j, w_in_k, 2 * j, i * (2 * N) + (C_RQ + (3 + u) * N))
            with sp.Fori(0, OUT_BLOCKS) as i:
                for j in range(8):
                    slot(i * 8 + S_UP, j, w_ur_k if j < 4 else w_ug_k, 2 * (j % 4), i * N)
            with sp.Fori(0, OUT_BLOCKS) as i:
                for j in range(8):
                    slot(i * 8 + S_OUT, j, w_out_k, 2 * j, i * N)
            with sp.Fori(0, FF_BLOCKS) as i:
                for j in range(16):
                    slot(i * 16 + S_FFN, j, w_fg_k if j < 8 else w_fu_k, 2 * (j % 8), i * N)
            for n in range(OUT_BLOCKS):
                for j in range(DOWN_SLOTS):
                    s = S_DOWN + n * DOWN_SLOTS + j
                    sp.wait_ge(w_low, s - RAW + 1)
                    sp.dma_start(raw[:, s % RAW, :, :], w_fd_k[:, 2 * j:2 * j + 2, n * N:(n + 1) * N])\
                      .then_inc(landed[s % RAW], 16)
            for m in range(MT):
                for n in range(OUT_BLOCKS):
                    sp.wait_ge(S("final_ready"), OUT_BLOCKS * m + n + 1)
                    sp.dma_start(out[m * P:(m + 1) * P, n * N:(n + 1) * N], y2[:, m, n * N:(n + 1) * N])\
                      .then_inc(S("out_stored"), 16)
            sp.wait_ge(S("out_stored"), 16 * MT * OUT_BLOCKS)

        def scale_pair(eng, k0):
            for k in (k0, k0 + 1):
                for e in range(2):
                    t = xr_t[:, k, e * L:(e + 1) * L]
                    last = eng.tensor_scalar(t, t, scale1[:, e, k:k + 1], mod_t[:, k, e:e + 1], ALU.mult, ALU.add)
            last.then_inc(S("h1_ready"), 1)

        def low_pair(eng, k):
            eng.wait_ge(S("h1_hi"), k // 2 + 1)
            for e, (lo, hi) in enumerate(((h_lo, h_hi), (hc_lo, hc_hi))):
                last = eng.tensor_tensor(lo[:, k:k + 2, :], xr_t[:, k:k + 2, e * L:(e + 1) * L],
                                         hi[:, k:k + 2, :].bitcast(F32), ALU.subtract)
            last.then_inc(S("h1_lo"), 1)

        @block.gpsimd
        def _(pool):
            for r0, n, v in ((0, 64, b_mod[2 * D:6 * D]), (64, 16, norm_mix_post), (80, 16, norm_ffn_post)):
                pool.dma_start(rows2[r0:r0 + n, :], v.rearrange("(r q) -> r q", q=P)).then_inc(S("rows2_landed"), 16)
            pool.dma_start(take[:, :], k_take).then_inc(S("rows2_landed"), 16)
            pool.dma_start(lg[:, :], ret_decay.rearrange("(a d) h -> a (d h)", a=1).broadcast_to([P, 2 * RH]))\
                .then_inc(S("consts_landed"), 16)
            pool.dma_start(mask_f[:, :, :], k_mask).then_inc(S("consts_landed"), 16)
            pool.memset(ones[:, :], 1.0).then_inc(S("ones_ready"), 1)
            pool.memset(minus_half[:, :], -0.5).then_inc(S("ones_ready"), 1)
            pool.wait_ge(S("ones_ready"), 2)
            pool.wait_ge(S("ssq_ready"), 1)
            pool.tensor_tensor(rstd[:, :], ssq[:, :], minus_half[:, :], ALU.pow).then_inc(S("rstd_ready"), 1)

            pool.wait_ge(S("mask_ready"), 1)
            pool.memset(a_up[:, :, :], 0.0).then_inc(S("gate_rows_set"), 1)
            pool.memset(al_t[:, :], 1.0).then_inc(S("gate_rows_set"), 1)
            pool.wait_ge(S("gate_rows_set"), 2)
            for d in range(2):
                for r in (d * LOW, (d + 2) * LOW):
                    pool.dma_start(a_up[r:r + LOW, d, :], gla_a_up[d]).then_inc(S("a_up_landed"), 16)
            pool.dma_start(a_up[4 * LOW:4 * LOW + 1, :, :], gla_a_bias.rearrange("(a d) n -> a d n", a=1))\
                .then_inc(S("a_up_landed"), 16)
            pool.wait_ge(S("xr_ready"), KT // 2)
            pool.wait_ge(S("xr_ready_odd"), KT // 2)
            for q in range(QUARTERS - 1):
                pool.wait_ge(S("scale1_ready"), 2 * q + 2)
                for k in (4 * q, 4 * q + 2):
                    scale_pair(pool, k)
                    low_pair(pool, k)
            pool.wait_ge(S("mod_cols_done"), MOD_BLOCKS)
            pool.dma_start(ga_w[:, :, :], w_in_k[:, :, C_GA:C_GA + 2 * LOW]).then_inc(S("ga_landed"), 16)
            pool.dma_start(rope[:, :, :, :], k_rope).then_inc(S("tables_landed"), 16)
            for t, k in ((before, k_before), (after, k_after)):
                pool.dma_start(t[:, :, :], k).then_inc(S("tables_landed"), 16)
            pool.wait_ge(S("tables_landed"), 16 * 3)
            for m in range(4):
                pool.wait_ge(stored[m], 16 * 5)
            pool.wait_ge(S("ga_done"), 1)
            pool.dma_start(gkc[:, :, :], pc_t[:, :, C_GK:C_GK + GH * GDK]).then_inc(S("gkc_landed"), 16)
            for d in range(2):
                pool.wait_ge(S("kw_ready"), d + 1)
                pool.dma_start(kwd[d].rearrange("(m p) n -> p m n", p=P), kw[:, d, :, :]).then_inc(S("kw_stored"), 16)
            pool.wait_ge(S("wm_used"), 4 * KT)
            pool.dma_start(accd.rearrange("g p n -> p g n"), acc[:, 1:4, :]).then_inc(S("acc_stored"), 16)
            pool.dma_start(dist[:, :, :, :], k_dist).then_inc(S("dist_landed"), 16)
            pool.wait_ge(S("lg_exp"), 1)
            pool.tensor_scalar(lg[:, :], lg[:, :], -1.0, None, ALU.mult).then_inc(S("lg_ready"), 1)
            pool.wait_ge(S("lg_ready"), 1)
            pool.wait_ge(S("dist_landed"), 16)
            pool.wait_ge(S("kw_stored"), 32)
            for h in range(RH):
                if h > 0:
                    pool.wait_ge(S("dist_sum"), h)
                pool.tensor_scalar(d_tmp[:, :, :], dist[:, 1, :, :], lg[:, RH + h:RH + h + 1], None, ALU.mult)\
                    .then_inc(S("dist_part"), 1)
                pool.tensor_scalar(dmat[:, h, 2:4, :], dist[:, 0, :, :], lg[:, h:h + 1], None, ALU.mult)\
                    .then_inc(S("dist_part"), 1)
                pool.wait_ge(S("dist_part"), 2 * h + 2)
                pool.tensor_tensor(dmat[:, h, 2:4, :], dmat[:, h, 2:4, :], d_tmp[:, :, :], ALU.add)\
                    .then_inc(S("dist_sum"), 1)
            pool.wait_ge(S("gw_rows_ready"), 1)
            pool.dma_start(gwd[0].rearrange("(r q) -> r q", q=P), gw_rows[:, :]).then_inc(S("gw_stored"), 16)

            def add_ctx_decay(h):
                pool.wait_ge(S("dctx_exp"), h + 1)
                pool.tensor_tensor(dmat[:, h, 0:2, :], dmat[:, h, 0:2, :], d_ctx[:, h, :, :], ALU.add)\
                    .then_inc(S("dctx_ready"), 1)

            def load(dst, src, col, name):
                pool.dma_start(dst, src[:, :, bass.ds(col, dst.shape[2])]).then_inc(S(name), 16)

            def load_g_qk(h):
                load(g_q[:, :, :], px_t, h * GDK + C_GQ, "g_qk_landed")
                load(g_k[:, :, :], px_t, h * GDK + C_GK, "g_qk_landed")

            def load_g_kw(h):
                for d in range(2):
                    load(g_kw[:, d, :, :], kwd[d].rearrange("(m p) n -> p m n", p=P), h * GDK, "g_v_landed")

            def load_r_kc(h):
                load(r_kc[:, :, :], pc_t, h * RDK + C_RK, "r_kc_landed")

            def load_r_qk(h):
                load(r_q[:, :, :], px_t, h * RDK + C_RQ, "r_qk_landed")
                load(r_k[:, :, :], px_t, h * RDK + C_RK, "r_qk_landed")

            def load_v(h):
                load(g_v[:, 0:2, :], pc_t, h * GDV + C_GV, "g_v_landed")
                load(g_v[:, 2:4, :], px_t, h * GDV + C_GV, "g_v_landed")
                load(r_v[:, 0:2, :], pc_t, h * RDK + C_RV, "r_v_landed")
                load(r_v[:, 2:4, :], px_t, h * RDK + C_RV, "r_v_landed")

            def load_r_gate(h):
                load(r_g[:, :, :], px_t, h * RDK + C_RG, "gates_landed")

            def load_g_gate(h):
                load(g_g[:, :, :], px_t, h * GDV + C_GG, "gates_landed")

            def head(i, last):
                pool.wait_ge(S("r_qk_landed"), i * 32 + 32)
                for n, t in enumerate((r_q, r_k)):
                    a, b = t[:, :, 0:P], t[:, :, P:2 * P]
                    for e, (u, f) in enumerate(((a, 0), (b, 1), (a, 1), (b, 0))):
                        pool.tensor_tensor(r_tmp[:, e, :, :], u, rope[:, f, :, :], ALU.mult)\
                            .then_inc(S("rope_prod"), 1)
                    pool.wait_ge(S("rope_prod"), i * 8 + (4 * n + 4))
                    pool.tensor_tensor(a, r_tmp[:, 0, :, :], r_tmp[:, 1, :, :], ALU.subtract).then_inc(S("rope_ready"), 1)
                    pool.tensor_tensor(b, r_tmp[:, 2, :, :], r_tmp[:, 3, :, :], ALU.add).then_inc(S("rope_ready"), 1)
                    pool.wait_ge(S("rope_ready"), i * 4 + (2 * n + 2))
                if not last:
                    pool.wait_ge(S("g_qk_turned"), i + 1)
                    load_g_qk(i + 1)
                    pool.wait_ge(S("g_state_done"), i + 1)
                    load_g_kw(i + 1)
                    pool.wait_ge(S("r_kc_turned"), i + 1)
                    load_r_kc(i + 1)
                    pool.wait_ge(S("r_qk_turned"), i + 1)
                    load_r_qk(i + 1)
                pool.wait_ge(S("r_var_ready"), i + 1)
                pool.tensor_tensor(hr[:, 0, :, :], mv[:, 0, :, 1:2],
                                   minus_half[:, 0:MT].rearrange("p (m o) -> p m o", o=1), ALU.pow)\
                    .then_inc(S("r_rstd_ready"), 1)
                pool.wait_ge(S("g_ms_ready"), i + 1)
                pool.tensor_tensor(hr[:, 1, :, :], mv[:, 1, :, 0:1],
                                   minus_half[:, 0:MT].rearrange("p (m o) -> p m o", o=1), ALU.pow)\
                    .then_inc(S("g_rstd_ready"), 1)
                if not last:
                    pool.wait_ge(S("r_o_done"), i + 1)
                    pool.wait_ge(S("g_o_done"), i + 1)
                    load_v(i + 1)
                    pool.wait_ge(S("r_on_turned"), i + 1)
                    load_r_gate(i + 1)
                    pool.wait_ge(S("g_on_turned"), i + 1)
                    pool.wait_ge(stored[0], 16 * 11)
                    pool.wait_ge(stored[1], 16 * 11)
                    load_g_gate(i + 1)

            for h in range(RH - 1):
                add_ctx_decay(h)
            for b, blocks in ((0, 10), (1, 10), (2, 9), (3, 9)):
                pool.wait_ge(stored[b], 16 * blocks)
            pool.wait_ge(S("acc_stored"), 16)
            load_g_qk(0)
            load_g_kw(0)
            load_r_qk(0)
            load_r_kc(0)
            load_v(0)
            load_r_gate(0)
            pool.wait_ge(stored[2], 16 * 10)
            pool.wait_ge(stored[3], 16 * 10)
            load_g_gate(0)
            add_ctx_decay(RH - 1)
            pool.wait_ge(S("gw_stored"), 16)
            with pool.Fori(0, RH - 1) as i:
                head(i, False)
            head(RH - 1, True)

            pool.wait_ge(S("gla_head_done"), RH + 1)
            pool.wait_ge(S("ret_head_done"), RH + 1)

            pool.wait_ge(stored[2], 16 * 12)
            pool.wait_ge(stored[3], 16 * 12)
            pool.wait_ge(stored[0], 16 * 14)
            pool.wait_ge(stored[1], 16 * 14)
            pool.dma_start(gate_s[:, 0, :, :], px_t[:, :, C_GATE_A:C_GATE_A + N]).then_inc(S("gate_landed0"), 16)
            pool.dma_start(gate_s[:, 1, :, :], px_t[:, :, C_GATE_A + D:C_GATE_A + D + N]).then_inc(S("gate_landed1"), 16)
            pool.wait_ge(stored[2], 16 * 14)
            pool.wait_ge(stored[3], 16 * 14)
            pool.wait_ge(stored[0], 16 * 15)
            pool.wait_ge(stored[1], 16 * 15)
            with pool.Fori(0, OUT_BLOCKS - 1) as i:
                for g in range(2):
                    pool.wait_ge(S(f"gate_used{g}"), i + 1)
                    pool.dma_start(gate_s[:, g, :, :], px_t[:, :, bass.ds(i * N + (C_GATE_A + g * D + N), N)])\
                        .then_inc(S(f"gate_landed{g}"), 16)
            pool.wait_ge(w_used, S_OUT)
            pool.dma_start(hs[:, :, :], x.rearrange("(m p) n -> p m n", p=P)).then_inc(S("res_landed"), 16)
            pool.dma_start(g1w[:, :], gwd[0:1, :].broadcast_to([P, D])).then_inc(S("res_landed"), 16)
            pool.dma_start(acc2[:, :, :], accd.rearrange("g p n -> p g n")).then_inc(S("acc_landed"), 16)
            pool.wait_ge(S("ssy_ready"), 2)
            pool.tensor_tensor(rstd[:, 0:MT], ssq[:, 0:MT], minus_half[:, 0:MT], ALU.pow).then_inc(S("rstd_ready"), 1)
            for m in range(MT):
                pool.wait_ge(S("hs_ready"), m + 1)
                pool.dma_start(hsd[m * P:(m + 1) * P, :], hs[:, m, :]).then_inc(S("hs_stored"), 16)
            pool.wait_ge(S("ssh_ready"), 1)
            pool.tensor_tensor(rstd[:, 2:4], ssq[:, 2:4], minus_half[:, 0:MT], ALU.pow).then_inc(S("rstd_ready"), 1)
            pool.wait_ge(S("gw_rows_ready"), 2)
            pool.dma_start(gwd[1].rearrange("(r q) -> r q", q=P), gw_rows[:, :]).then_inc(S("gw_stored"), 16)
            pool.wait_ge(S("gw_stored"), 32)
            pool.wait_ge(S("hs_stored"), 16 * MT)
            pool.wait_ge(w_used, S_DOWN)
            pool.wait_ge(S("hid_n_ready"), FF_BLOCKS)
            pool.dma_start(hs2[:, :, :], hsd.rearrange("(m p) n -> p m n", p=P)).then_inc(S("end_landed"), 16)
            pool.dma_start(g2w[:, :], gwd[1:2, :].broadcast_to([P, D])).then_inc(S("end_landed"), 16)
            pool.wait_ge(S("ssy_ready"), 4)
            pool.tensor_tensor(rstd[:, 0:MT], ssq[:, 0:MT], minus_half[:, 0:MT], ALU.pow).then_inc(S("rstd_ready"), 1)

        @block.scalar
        def _(act):
            def split(s, j):
                if isinstance(s, int):
                    s, j = 0, s + j
                    act.wait_ge(landed[j % RAW], 16 * (j // RAW + 1))
                else:
                    act.wait_ge(landed[j % RAW], s * 2 + 16 * (j // RAW + 1))
                if not isinstance(s, int) or j >= SPLIT:
                    act.wait_ge(w_used, s + (j - SPLIT + 1))
                act.activation(w_hi[:, j % SPLIT, :, :], raw[:, j % RAW, :, :], ACT.Copy).then_inc(w_high, 1)

            def stage_ctx(b, group):
                act.wait_ge(w_used, b * 8 + (S_CTX + 8))
                for m in range(4):
                    if not isinstance(b, int) or b > 0:
                        act.wait_ge(stored[m], b * 16)
                    act.activation(stage[:, m, :], bank(4 * group + m), ACT.Copy).then_inc(staged[m], 1)

            def store_ctx(b):
                for m in range(4):
                    act.wait_ge(staged[m], b + 1)
                    act.dma_start((px if m < 2 else pc)[m % 2 * P:(m % 2 + 1) * P, bass.ds(b * N, N)], stage[:, m, :])\
                        .then_inc(stored[m], 16)

            def store_lat(i, t):
                for m in range(2):
                    b = 2 * (t % 2) + m
                    act.wait_ge(staged[b], i + (CTX_BLOCKS + t // 2 + 1))
                    act.dma_start(px[m * P:(m + 1) * P, bass.ds(i * (2 * N) + (C_RQ + t * N), N)], stage[:, b, :])\
                        .then_inc(stored[b], 16)

            def stage_lat(i, t):
                act.wait_ge(w_used, i * 16 + (S_LAT + 8 * (t + 1)))
                for m in range(2):
                    b = 2 * (t % 2) + m
                    act.wait_ge(stored[b], i * 16 + 16 * (CTX_BLOCKS + t // 2))
                    act.activation(stage[:, b, :], bank(b), ACT.Copy).then_inc(staged[b], 1)

            def load_chunk(i, n, g, k):
                if not isinstance(i, int) or n >= 2:
                    act.wait_ge(S("wm_used"), i * 16 + (n - 1))
                act.dma_start(wm[:, n % 2, :], w_mod_k[:, k, bass.ds(i * D + (2 + g) * D, D)])\
                    .then_inc(S(f"wm_landed{n % 2}"), 16)

            act.wait_ge(S("cols_turned"), 1)
            act.activation(csil[:, :], bank(7)[:, 0:2 * KT], ACT.Silu).then_inc(S("cols_ready"), 1)
            act.wait_ge(S("cols_ready"), 1)
            act.activation(c4[:, 0:2, :], csil[:, :].rearrange("p (s k) -> p s k", s=2), ACT.Copy).then_inc(S("cols_ready"), 1)
            act.activation(cols[:, :], bank(7)[:, 0:112], ACT.Copy).then_inc(S("cols_ready"), 1)
            act.wait_ge(S("cols_turned"), 2)
            act.activation(cols2[:, :], bank(6)[:, 0:96], ACT.Copy).then_inc(S("cols_ready"), 1)

            for m in range(4):
                act.wait_ge(S(f"x_landed{m}"), 16)
                if m > 0:
                    act.wait_ge(S("square"), m)
                act.activation(junk0[:, :], xn[:, m, :], ACT.Square, accum_out=ssq[:, m:m + 1]).then_inc(S("square"), 1)

            def take_mod_row(n):
                act.wait_ge(w_used, mod_end[n] + 1)
                act.activation(mod_row[:, n, :], bank(4 + n % 2)[0:4, :], ACT.Copy).then_inc(S("mod_row_ready"), 1)

            def high_pair(k):
                act.wait_ge(S("h1_ready"), k // 2 + 1)
                act.activation(h_hi[:, k:k + 2, :], xr_t[:, k:k + 2, 0:L], ACT.Copy)
                act.activation(hc_hi[:, k:k + 2, :], xr_t[:, k:k + 2, L:2 * L], ACT.Copy).then_inc(S("h1_hi"), 1)

            for s in range(len(opening)):
                if s == 7:
                    act.wait_ge(S("consts_landed"), 16 * 2)
                    act.activation(lg[:, :], lg[:, :], ACT.Exp).then_inc(S("lg_exp"), 1)
                if s in XR_AT:
                    k = 2 * XR_AT.index(s) + 1
                    act.wait_ge(S("x_turned"), k + 1)
                    act.activation(xr_t[:, k, :], bank(k % 4), ACT.Copy).then_inc(S("xr_ready_odd"), 1)
                if s - 5 in mod_end:
                    take_mod_row(mod_end.index(s - 5))
                if s - 4 in H1_AT:
                    high_pair(4 * H1_AT.index(s - 4))
                if s - 8 in H1_AT:
                    high_pair(4 * H1_AT.index(s - 8) + 2)
                split(s, 0)
            take_mod_row(MOD_BLOCKS - 1)
            high_pair(KT - 4)
            high_pair(KT - 2)
            act.wait_ge(S("mod_cols_done"), MOD_BLOCKS)
            load_chunk(0, 0, 0, 0)
            for j in range(8):
                if j == 4:
                    stage_ctx(0, 0)
                if j == 5:
                    store_ctx(0)
                split(S_CTX + 8, j)
                load_chunk(0, j + 1, 0, j + 1)
            with act.Fori(0, 2) as i:
                for u in range(2):
                    for j in range(8):
                        if j == 4:
                            stage_ctx(i * 2 + (1 + u), 1 - u)
                        if j == 5:
                            store_ctx(i * 2 + (1 + u))
                        split(i * 16 + (S_CTX + 16 + 8 * u), j)
                        n = 8 + 8 * u + j + 1
                        load_chunk(i, n, *chunk_of(n))
            for j in range(8):
                if j == 4:
                    stage_ctx(5, 1)
                if j == 5:
                    store_ctx(5)
                split(S_CTX + 48, j)
                load_chunk(0, 40 + j + 1, *chunk_of(40 + j + 1))
            act.wait_ge(S("ga_landed"), 16)
            act.activation(ga_hl[:, :, 0, :], ga_w[:, :, :], ACT.Copy).then_inc(S("ga_hi_ready"), 1)

            def at_pre(p):
                if p == 3:
                    act.wait_ge(S("ga_done"), 1)
                    act.wait_ge(S("gate_rows_set"), 2)
                    act.activation(al_t[0:4 * LOW, :], bank(4)[0:4 * LOW, :], ACT.Copy).then_inc(S("al_ready"), 1)
                if p in (5, 6, 7, 11, 12, 13):
                    d, step = divmod(p - 5, 6)
                    t = la[:, d, :, :].rearrange("p m n -> p (m n)")
                    if step == 0:
                        act.wait_ge(S("z_done"), d + 1)
                        act.activation(t, bank(4, 4), ACT.Abs).then_inc(S("la_step"), 1)
                    else:
                        act.wait_ge(S("la_step"), 3 * d + step)
                        if step == 1:
                            act.activation(t, t, ACT.Exp, scale=-1.0).then_inc(S("la_step"), 1)
                        else:
                            act.activation(t, t, ACT.Ln, bias=1.0).then_inc(S("la_step"), 1)
                if p in (17, 18):
                    d = p - 17
                    act.wait_ge(S("sums_done"), d + 1)
                    act.activation(cum[:, d, :, :], bank(4, 4).rearrange("p (h n) -> p h n", h=GH)[:, :, 0:L + 1],
                                   ACT.Copy).then_inc(S("cum_ready"), 1)
                if p in (19, 20):
                    d = p - 19
                    act.wait_ge(S("ctx_sums_done"), d + 1)
                    act.activation(kw[:, d, :, :], bank(4 + 2 * d, 2).rearrange("p (m n) -> p m n", m=MT), ACT.Exp,
                                   scale=1.0 / GATE_NORM).then_inc(S("kw_exp"), 1)
                if p == 43:
                    act.wait_ge(S("gw_turned"), 1)
                    act.activation(gw_rows[:, :], bank(5)[0:KT, 0:P], ACT.Copy).then_inc(S("gw_rows_ready"), 1)
                if p in (40, 42, 44, 46):
                    h = (p - 40) // 2
                    if h == 0:
                        act.wait_ge(S("kw_stored"), 32)
                    act.wait_ge(S("dist_sum"), h + 1)
                    act.activation(dmat[:, h, 2:4, :], dmat[:, h, 2:4, :], ACT.Exp)
                    act.activation(dmat[:, h, 0:2, :], dist[:, 2, :, :], ACT.Exp, scale=lg[:, h:h + 1])
                    act.activation(d_ctx[:, h, :, :], dist[:, 3, :, :], ACT.Exp, scale=lg[:, RH + h:RH + h + 1])\
                        .then_inc(S("dctx_exp"), 1)

            for t in range(7):
                for j in range(8):
                    if j == 0 and t == 0:
                        stage_ctx(6, 0)
                    if j == 1 and t == 0:
                        store_ctx(6)
                    if j == 4 and t > 0:
                        stage_lat(0, t - 1)
                    if j == 5 and t > 0:
                        store_lat(0, t - 1)
                    at_pre(8 * t + j)
                    split(S_LAT + 8 * t, j)
                    n = late_chunk(8 * t + j)
                    if n is not None and n + 1 < 4 * KT:
                        load_chunk(0, n + 1, *chunk_of(n + 1))
            with act.Fori(0, RH) as i:
                for p in range(16):
                    if p in (4, 12):
                        stage_lat(i, 6 + (p - 4) // 8)
                    if p in (5, 13):
                        store_lat(i, 6 + (p - 4) // 8)
                    if p == 1:
                        act.wait_ge(S("g_qk_turned"), i + 1)
                        act.activation(g_qkt[:, 0, :], bank(6)[:, 0:L], ACT.Copy, scale=GDK ** -0.5)\
                            .then_inc(S("g_qkt_ready"), 1)
                        act.activation(g_qkt[:, 1, :], bank(6)[:, L:2 * L], ACT.Copy).then_inc(S("g_qkt_ready"), 1)
                        act.wait_ge(S("g_st_arg"), i + 1)
                        act.activation(g_st[:, 1, :], g_st[:, 1, :], ACT.Exp, scale=1.0 / GATE_NORM)\
                            .then_inc(S("g_st_exp"), 1)
                        act.activation(g_st[:, 0:1, :], cum[:, 0, bass.ds(i, 1), 1:L + 1], ACT.Exp, scale=1.0 / GATE_NORM)\
                            .then_inc(S("g_st_exp"), 1)
                    if p in (2, 6):
                        act.wait_ge(S("g_arg_ready"), i * 2 + (1 + p // 4))
                        act.activation(g_arg[:, :, :, :], g_arg[:, :, :, :], ACT.Exp, scale=1.0 / GATE_NORM)\
                            .then_inc(S("g_exp_ready"), 1)
                    if p == 3:
                        act.wait_ge(S("g_state_done"), i + 1)
                        act.activation(g_s[:, :, :], bank(6).rearrange("p (d n) -> p d n", d=2), ACT.Copy)\
                            .then_inc(S("g_s_ready"), 1)
                    if p == 4:
                        act.wait_ge(S("r_kc_turned"), i + 1)
                        act.activation(r_kt[:, 0:2, :], bank(4).rearrange("p (f n) -> p f n", f=2), ACT.Copy)\
                            .then_inc(S("r_kct_ready"), 1)
                    if p == 7:
                        act.wait_ge(S("r_qk_turned"), i + 1)
                        act.activation(r_qt[:, :, :], bank(5).rearrange("p (f n) -> p f n", f=2), ACT.Copy,
                                       scale=RDK ** -0.5).then_inc(S("r_qkt_ready"), 1)
                        act.activation(r_kt[:, 2:4, :], bank(4).rearrange("p (f n) -> p f n", f=2), ACT.Copy)\
                            .then_inc(S("r_qkt_ready"), 1)
                    if p == 9:
                        act.wait_ge(S("g_levels_done"), i * 2 + 2)
                        act.activation(g_a[:, 2:4, :], bank(7)[:, L:2 * L].rearrange("p (a n) -> p a n", a=2), ACT.Copy)\
                            .then_inc(S("g_cross_ready"), 1)
                    if p == 10:
                        act.wait_ge(S("gates_landed"), i * 32 + 32)
                        act.activation(g_g[:, :, :], g_g[:, :, :], ACT.Silu).then_inc(S("g_silu"), 1)
                        act.activation(r_g[:, :, :], r_g[:, :, :], ACT.Silu).then_inc(S("r_silu"), 1)
                    split(i * 16 + (S_LAT + 8 * 7), p)

            for g in range(2):
                act.wait_ge(S("ret_head_done" if g == 0 else "gla_head_done"), RH + 1)
                act.activation(o_hi[:, g, :, :], o_t[:, g, :, :], ACT.Copy).then_inc(S("o_hi_ready"), 1)

            def turn_merged(n):
                act.wait_ge(S("turned"), n + 1)
                act.activation(h_hi[:, bass.ds(n * 4, 4), :], bank(4, 2).rearrange("p (q n) -> p q n", q=4), ACT.Copy)\
                    .then_inc(S("turned_hi"), 1)

            def up_block(s, n, prev):
                for j in range(8):
                    if j == 4 and prev is None:
                        stage_lat(0, 14)
                    if j == 5 and prev is None:
                        store_lat(0, 14)
                    if j == 6 and prev is not None:
                        turn_merged(prev)
                    if j >= 6:
                        g = j - 6
                        act.wait_ge(S(f"gate_landed{g}"), n * 16 + 16)
                        act.activation(gate_s[:, g, :, :], gate_s[:, g, :, :], ACT.Sigmoid).then_inc(S(f"gate_ready{g}"), 1)
                    split(s, j)
            up_block(S_UP, 0, None)
            with act.Fori(0, OUT_BLOCKS - 1) as i:
                up_block(i * 8 + (S_UP + 8), i + 1, i)

            def square_y(n, jk, slots, first):
                pair = 1 - n % 2
                act.wait_ge(w_used, slots)
                for m in range(MT):
                    if first + n + m > 0:
                        act.wait_ge(S("y_square"), 2 * (first + n) + m)
                    act.activation(jk[:, 0:N], bank(2 * pair + m), ACT.Square, accum_out=ssy[:, m, n:n + 1])\
                        .then_inc(S("y_square"), 1)

            for n in range(OUT_BLOCKS):
                for j in range(8):
                    if n == 0 and j == 6:
                        turn_merged(OUT_BLOCKS - 1)
                    if n > 0 and j == 4:
                        square_y(n - 1, junk, S_OUT + 8 * n, 0)
                    split(S_OUT + 8 * n, j)
            for j in range(4):
                split(S_FFN, j)
            square_y(OUT_BLOCKS - 1, junk, S_FFN, 0)
            for m in range(MT):
                act.wait_ge(S("hs_ready"), m + 1)
                act.wait_ge(S("square"), 4 + m)
                act.activation(junk[:, :], hs[:, m, :], ACT.Square, accum_out=ssq[:, 2 + m:3 + m]).then_inc(S("square"), 1)

            def turn_hidden(n):
                act.wait_ge(S("turned"), n + (OUT_BLOCKS + 1))
                act.activation(hid_hi[:, bass.ds(n * 4, 4), :], bank(4, 2).rearrange("p (q n) -> p q n", q=4), ACT.Copy)\
                    .then_inc(S("turned_hi"), 1)

            def ffn_block(s, n, prev):
                for j in range(16):
                    if prev is None and j < 8:
                        act.wait_ge(S("h2_turned"), j + 1)
                        if j >= 2:
                            act.wait_ge(S("h2_lo_ready"), j - 1)
                        for e in range(2):
                            k = 2 * j + e
                            act.activation(h2f[:, j % 2, e, :], bank(4 + j % 4)[:, e * L:(e + 1) * L], ACT.Identity,
                                           scale=mod2[:, 1, k:k + 1], bias=mod2[:, 0, k:k + 1]).then_inc(S("h2f_ready"), 1)
                        act.wait_ge(S("h2f_ready"), 2 * j + 2)
                        act.activation(h_hi[:, 2 * j:2 * j + 2, :], h2f[:, j % 2, :, :], ACT.Copy).then_inc(S("h2_hi_ready"), 1)
                    if prev is not None and j == 6:
                        turn_hidden(prev)
                    if j == 12:
                        act.wait_ge(w_used, n * 16 + (S_FFN + 8))
                        if prev is not None:
                            act.wait_ge(S("hid_n_ready"), n)
                        act.activation(sg[:, :, :], bank(2, 2).rearrange("p (m n) -> p m n", m=MT), ACT.Silu)\
                            .then_inc(S("silu_ready"), 1)
                    if prev is None and j == 15:
                        act.wait_ge(S("gw_turned"), 2)
                        act.wait_ge(S("gw_stored"), 16)
                        act.activation(gw_rows[:, :], bank(6)[0:KT, 0:P], ACT.Copy).then_inc(S("gw_rows_ready"), 1)
                    if prev is not None or j >= 4:
                        split(s, j)
            ffn_block(S_FFN, 0, None)
            act.wait_ge(S("hs_stored"), 16 * MT)
            with act.Fori(0, FF_BLOCKS - 1) as i:
                ffn_block(i * 16 + (S_FFN + 16), i + 1, i)
            for n in range(OUT_BLOCKS):
                for j in range(DOWN_SLOTS):
                    if n == 0 and j == 6:
                        turn_hidden(FF_BLOCKS - 1)
                    if n > 0 and j == 4:
                        square_y(n - 1, junk2, S_DOWN + n * DOWN_SLOTS, OUT_BLOCKS)
                    split(S_DOWN + n * DOWN_SLOTS, j)
            square_y(OUT_BLOCKS - 1, junk2, S_DOWN + OUT_BLOCKS * DOWN_SLOTS, OUT_BLOCKS)

        @block.vector
        def _(dve):
            def split(s, j):
                if isinstance(s, int):
                    s, j = 0, s + j
                dve.wait_ge(w_high, s + (j + 1))
                dve.tensor_tensor(w_lo[:, j % SPLIT, :, :], raw[:, j % RAW, :, :],
                                  w_hi[:, j % SPLIT, :, :].bitcast(F32), ALU.subtract).then_inc(w_low, 1)

            def add_chunk(i, n, g, k):
                b = n % 2
                a = acc[:, bass.ds(i + g, 1), :].rearrange("p o n -> p (o n)")
                dve.wait_ge(S(f"wm_landed{b}"), i * 128 + 16 * (n // 2 + 1))
                if k == 0:
                    dve.tensor_scalar(a, wm[:, b, :], csil[:, k:k + 1], None, ALU.mult).then_inc(S("wm_used"), 1)
                else:
                    dve.wait_ge(S("wm_used"), i * 16 + n)
                    dve.scalar_tensor_tensor(out=a, in0=wm[:, b, :], scalar=csil[:, k:k + 1], in1=a,
                                             op0=ALU.mult, op1=ALU.add).then_inc(S("wm_used"), 1)

            dve.memset(hr[:, 0, 0:1, :], 0.0).then_inc(S("ret_head_done"), 1)
            dve.memset(hr[:, 1, 0:1, :], 0.0).then_inc(S("gla_head_done"), 1)
            dve.wait_ge(S("cols_ready"), 2)
            dve.tensor_tensor(c4[:, 2:4, :], csil[:, :].rearrange("p (s k) -> p s k", s=2), c4[:, 0:2, :].bitcast(F32),
                              ALU.subtract).then_inc(S("c4_ready"), 1)

            dve.wait_ge(S("square"), 4)
            dve.tensor_scalar(ssq[:, :], ssq[:, :], 1.0 / D, EPS, ALU.mult, ALU.add).then_inc(S("ssq_ready"), 1)
            dve.wait_ge(S("rstd_ready"), 1)
            for m in range(4):
                dve.tensor_scalar(diag0[:, m, :], ident[:, :], rstd[:, m:m + 1], None, ALU.mult).then_inc(S("diag_ready"), 1)

            def modulate(q):
                dve.wait_ge(S("cols_ready"), 3)
                dve.wait_ge(S("mod_cols_done"), 2 * q + 2)
                for a in range(2):
                    k = slice(a * KT + 4 * q, a * KT + 4 * q + 4)
                    dve.tensor_tensor(mod_t[:, k, :], bank(6)[:, 0:64].rearrange("p (k s) -> p k s", s=2)[:, k, :],
                                      cols[:, 80:112].rearrange("p (k o) -> p k o", o=1)[:, k, :].broadcast_to([P, 4, 2]),
                                      ALU.add).then_inc(S("mod_ready"), 1)
                dve.wait_ge(S("mod_ready"), 2 * q + 2)
                for e in range(2):
                    dve.scalar_tensor_tensor(out=scale1[:, e, 4 * q:4 * q + 4], in0=mod_t[:, KT + 4 * q:KT + 4 * q + 4, e],
                                             scalar=1.0, in1=cols[:, 2 * KT + 4 * q:2 * KT + 4 * q + 4],
                                             op0=ALU.add, op1=ALU.mult).then_inc(S("scale1_ready"), 1)
                dve.wait_ge(S("scale1_ready"), 2 * q + 2)

            for s in range(len(opening)):
                if s == 14:
                    dve.wait_ge(S("consts_landed"), 16 * 2)
                    dve.tensor_copy(mask[:, :, :], mask_f[:, :, :]).then_inc(S("mask_ready"), 1)
                if s in XR_AT:
                    k = 2 * XR_AT.index(s)
                    dve.wait_ge(S("x_turned"), k + 1)
                    dve.tensor_copy(xr_t[:, k, :], bank(k % 4)).then_inc(S("xr_ready"), 1)
                if s in H1_AT:
                    modulate(H1_AT.index(s))
                split(s, 0)
            modulate(QUARTERS - 1)
            dve.wait_ge(S("h1_lo"), KT // 2 - 2)
            for k in (KT - 4, KT - 2):
                scale_pair(dve, k)
            for k in (KT - 4, KT - 2):
                low_pair(dve, k)
            dve.wait_ge(S("h1_lo"), KT // 2)
            for j in range(8):
                add_chunk(0, j, 0, j)
                split(S_CTX + 8, j)
            with dve.Fori(0, 2) as i:
                for u in range(2):
                    for j in range(8):
                        n = 8 + 8 * u + j
                        add_chunk(i, n, *chunk_of(n))
                        split(i * 16 + (S_CTX + 16 + 8 * u), j)
            for j in range(8):
                add_chunk(0, 40 + j, *chunk_of(40 + j))
                split(S_CTX + 48, j)
            dve.wait_ge(S("ga_hi_ready"), 1)
            dve.tensor_tensor(ga_hl[:, :, 1, :], ga_w[:, :, :], ga_hl[:, :, 0, :].bitcast(F32), ALU.subtract)\
                .then_inc(S("ga_lo_ready"), 1)

            def at_pre(p):
                if p in (8, 14):
                    d = (p - 8) // 6
                    t = la[:, d, :, :].rearrange("p m n -> p (m n)")
                    dve.wait_ge(S("la_step"), 3 * d + 3)
                    dve.scalar_tensor_tensor(out=t, in0=bank(4, 4), scalar=0.0, in1=t, op0=ALU.min, op1=ALU.subtract)\
                        .then_inc(S("la_ready"), 1)
                if p in (20, 21):
                    d = p - 20
                    dve.wait_ge(S("kw_exp"), d + 1)
                    dve.wait_ge(S("gkc_landed"), 16)
                    dve.tensor_tensor(kw[:, d, :, :], kw[:, d, :, :], gkc[:, :, :], ALU.mult).then_inc(S("kw_ready"), 1)
                if p == 39:
                    gate_weight(0, bank(4), 1)

            def gate_weight(d, src, done):
                dve.wait_ge(S("partitions_added"), done)
                dve.tensor_tensor(gw_cols[:, d, :], src[:, 0:KT], cols2[:, 48 * d:48 * d + KT], ALU.add)\
                    .then_inc(S("mod2_part"), 1)
                dve.wait_ge(S("mod2_part"), 1 + 4 * d)
                dve.tensor_tensor(gw_cols[:, d, :], gw_cols[:, d, :], cols2[:, (4 + d) * KT:(5 + d) * KT], ALU.mult)\
                    .then_inc(S("mod2_part"), 1)

            for t in range(7):
                for j in range(8):
                    at_pre(8 * t + j)
                    n = late_chunk(8 * t + j)
                    if n is not None:
                        add_chunk(0, n, *chunk_of(n))
                    split(S_LAT + 8 * t, j)
            def exponents(i, first):
                for e in range(4):
                    h = LEVELS[first + e]
                    n = L // (2 * h)

                    def view(d, a):
                        return cum[:, d, bass.ds(i, 1), a:a + L].rearrange("p o (b u e) -> p (o b) u e", u=2, e=h)

                    def mid(d):
                        return view(d, 0)[:, :, 1, 0:1].broadcast_to([P, n, h])

                    q = g_arg[:, 0, e, :].rearrange("p (b u e) -> p b u e", u=2, e=h)
                    k = g_arg[:, 1, e, :].rearrange("p (b u e) -> p b u e", u=2, e=h)
                    dve.tensor_tensor(q[:, :, 1, :], view(0, 1)[:, :, 1, :], mid(0), ALU.subtract)
                    dve.tensor_tensor(q[:, :, 0, :], mid(1), view(1, 0)[:, :, 0, :], ALU.subtract)
                    dve.tensor_tensor(k[:, :, 0, :], mid(0), view(0, 1)[:, :, 0, :], ALU.subtract)
                    last = dve.tensor_tensor(k[:, :, 1, :], view(1, 0)[:, :, 1, :], mid(1), ALU.subtract)
                last.then_inc(S("g_arg_ready"), 1)

            def hold(n):
                dve.memset(spare[:, n:n + 1], 0.0)

            def weigh(i, r):
                dve.wait_ge(S("g_exp_ready"), i * 2 + (r + 1))
                for a in range(2):
                    last = dve.tensor_tensor(g_arg[:, a, :, :], g_arg[:, a, :, :],
                                             g_qkt[:, a:a + 1, :].broadcast_to([P, 4, L]), ALU.mult)
                last.then_inc(S("g_qk_ready"), 1)

            def pick(i, r, n):
                dve.wait_ge(S("g_levels_done"), i * 2 + (r + 1))
                if r == 1:
                    dve.wait_ge(S("g_cross_ready"), i + 1)
                for e in range(n):
                    if r == 1 or e > 0:
                        dve.wait_ge(S("g_picked"), i * 7 + (4 * r + e))
                    else:
                        dve.wait_ge(S("g_diag_ready"), i + 1)
                    hold(4 * r + e)
                    src = bank(6, 2)[:, e * L:(e + 1) * L].rearrange("p (a n) -> p a n", a=2)
                    dve.copy_predicated(g_a[:, 0:2, :],
                                        mask[:, 4 * r + e:4 * r + e + 1, :].broadcast_to([P, 2, P]), src)\
                        .then_inc(S("g_picked"), 1)

            dve.wait_ge(S("dctx_ready"), RH)
            with dve.Fori(0, RH) as i:
                for p in range(16):
                    if p == 0:
                        exponents(i, 0)
                        dve.tensor_tensor(g_st[:, 1:2, :], cum[:, 1, bass.ds(i, 1), L:L + 1].broadcast_to([P, 1, L]),
                                          cum[:, 1, bass.ds(i, 1), 0:L], ALU.subtract).then_inc(S("g_st_arg"), 1)
                    if p == 3:
                        dve.wait_ge(S("g_qkt_ready"), i * 2 + 2)
                        weigh(i, 0)
                        dve.wait_ge(S("g_st_exp"), i * 2 + 2)
                        dve.tensor_tensor(g_st[:, :, :], g_st[:, :, :], g_qkt[:, 0:1, :].broadcast_to([P, 2, L]), ALU.mult)\
                            .then_inc(S("g_st_ready"), 1)
                        dve.wait_ge(S("g_diag_done"), i + 1)
                        dve.tensor_tensor(g_a[:, 0:2, :], bank(7)[:, 0:L].rearrange("p (a n) -> p a n", a=2),
                                          ident[:, :].rearrange("p (o n) -> p o n", o=1).broadcast_to([P, 2, P]),
                                          ALU.mult).then_inc(S("g_diag_ready"), 1)
                    if p == 5:
                        pick(i, 0, 4)
                        exponents(i, 4)
                    if p == 7:
                        weigh(i, 1)
                    if p == 8:
                        dve.wait_ge(S("r_scores_done"), i + 1)
                        dve.tensor_tensor(r_a[:, :, :], bank(4, 2).rearrange("p (a n) -> p a n", a=4),
                                          dmat[:, bass.ds(i, 1), :, :].rearrange("p o a n -> p (o a) n"), ALU.mult)\
                            .then_inc(S("r_a_ready"), 1)
                    if p == 10:
                        pick(i, 1, 3)
                        dve.wait_ge(S("r_o_done"), i + 1)
                        for m in range(MT):
                            dve.bn_stats(stats[:, 0, m, :], bank(4)[:, m * RDK:(m + 1) * RDK]).then_inc(S("r_stat"), 1)
                        dve.wait_ge(S("r_stat"), i * 4 + 2)
                        hold(8)
                        for m in range(MT):
                            dve.bn_aggr(mv[:, 0, m, :], stats[:, 0, m, :]).then_inc(S("r_stat"), 1)
                        dve.wait_ge(S("r_stat"), i * 4 + 4)
                        dve.tensor_scalar(mv[:, 0, :, 1:2], mv[:, 0, :, 1:2], EPS, None, ALU.add)\
                            .then_inc(S("r_var_ready"), 1)
                    if p == 11:
                        dve.wait_ge(S("g_o_done"), i + 1)
                        for m in range(MT):
                            dve.bn_stats(stats[:, 1, m, :], bank(6)[:, m * GDV:(m + 1) * GDV]).then_inc(S("g_stat"), 1)
                        dve.wait_ge(S("g_stat"), i * 5 + 2)
                        hold(7)
                        for m in range(MT):
                            dve.bn_aggr(mv[:, 1, m, :], stats[:, 1, m, :]).then_inc(S("g_stat"), 1)
                        dve.wait_ge(S("g_stat"), i * 5 + 4)
                        dve.tensor_tensor(mv[:, 1, :, 0:1], mv[:, 1, :, 0:1], mv[:, 1, :, 0:1], ALU.mult)\
                            .then_inc(S("g_stat"), 1)
                        dve.wait_ge(S("g_stat"), i * 5 + 5)
                        dve.scalar_tensor_tensor(out=mv[:, 1, :, 0:1], in0=mv[:, 1, :, 0:1], scalar=EPS,
                                                 in1=mv[:, 1, :, 1:2], op0=ALU.add, op1=ALU.add)\
                            .then_inc(S("g_ms_ready"), 1)
                    if p == 12:
                        dve.wait_ge(S("r_silu"), i + 1)
                        for m in range(MT):
                            dve.scalar_tensor_tensor(out=r_g[:, m, :], in0=bank(4)[:, m * RDK:(m + 1) * RDK],
                                                     scalar=mv[:, 0, m, 0:1], in1=r_g[:, m, :],
                                                     op0=ALU.subtract, op1=ALU.mult).then_inc(S("r_centred"), 1)
                        dve.wait_ge(S("r_rstd_ready"), i + 1)
                        dve.wait_ge(S("r_centred"), i * 2 + 2)
                        for m in range(MT):
                            last = dve.tensor_scalar(r_g[:, m, :], r_g[:, m, :], hr[:, 0, m, :], None, ALU.mult)
                        last.then_inc(S("r_on_ready"), 1)
                    if p == 13:
                        dve.wait_ge(S("g_rstd_ready"), i + 1)
                        dve.wait_ge(S("g_silu"), i + 1)
                        for m in range(MT):
                            last = dve.scalar_tensor_tensor(out=g_g[:, m, :], in0=bank(6)[:, m * GDV:(m + 1) * GDV],
                                                            scalar=hr[:, 1, m, :], in1=g_g[:, m, :],
                                                            op0=ALU.mult, op1=ALU.mult)
                        last.then_inc(S("g_on_ready"), 1)
                    if p == 14:
                        dve.wait_ge(S("r_on_turned"), i + 1)
                        dve.tensor_tensor(o_t[:, 0, bass.ds(i * 2, 2), :], bank(5).rearrange("p (a n) -> p a n", a=2),
                                          cols[:, bass.ds(i * 2 + 64, 2)].rearrange("p (a o) -> p a o", o=1)
                                          .broadcast_to([P, 2, L]), ALU.mult).then_inc(S("ret_head_done"), 1)
                    if p == 15:
                        dve.wait_ge(S("g_on_turned"), i + 1)
                        dve.tensor_tensor(o_t[:, 1, bass.ds(i * 2, 2), :], bank(7).rearrange("p (a n) -> p a n", a=2),
                                          cols[:, bass.ds(i * 2 + 72, 2)].rearrange("p (a o) -> p a o", o=1)
                                          .broadcast_to([P, 2, L]), ALU.mult).then_inc(S("gla_head_done"), 1)
                    split(i * 16 + (S_LAT + 8 * 7), p)

            for g in range(2):
                dve.wait_ge(S("o_hi_ready"), g + 1)
                dve.tensor_tensor(o_lo[:, g, :, :], o_t[:, g, :, :], o_hi[:, g, :, :].bitcast(F32), ALU.subtract)\
                    .then_inc(S("o_lo_ready"), 1)

            def merge(j, n):
                if j in (0, 4):
                    g = j // 4
                    dve.wait_ge(w_used, n * 8 + (S_UP + 4 + 4 * g))
                    dve.wait_ge(S(f"gate_ready{g}"), n + 1)
                    dve.tensor_tensor(up_t[:, g, :, :], bank(2 - 2 * g, 2).rearrange("p (m n) -> p m n", m=MT),
                                      gate_s[:, g, :, :], ALU.mult).then_inc(S(f"gate_used{g}"), 1)
                if j == 4:
                    dve.wait_ge(S("gate_used0"), n + 1)
                    dve.wait_ge(S("gate_used1"), n + 1)
                    dve.tensor_tensor(mg[:, :, :], up_t[:, 0, :, :], up_t[:, 1, :, :], ALU.add).then_inc(S("mg_ready"), 1)
                if j == 6:
                    hh = bass.ds(n * 4, 4)
                    dve.wait_ge(S("turned_hi"), n + 1)
                    dve.tensor_tensor(h_lo[:, hh, :], bank(4, 2).rearrange("p (q n) -> p q n", q=4),
                                      h_hi[:, hh, :].bitcast(F32), ALU.subtract).then_inc(S("turned_lo"), 1)

            for j in range(8):
                split(S_UP, j)
            with dve.Fori(0, OUT_BLOCKS - 1) as i:
                for j in range(8):
                    merge(j, i)
                    split(i * 8 + (S_UP + 8), j)
            def scale_y(n, yy, w, first):
                pair = 1 - n % 2
                dve.wait_ge(S("y_square"), 2 * (first + n + 1))
                if first + n == 0:
                    dve.wait_ge(S("res_landed"), 32)
                if first > 0 and n == 0:
                    dve.wait_ge(S("end_landed"), 32)
                dve.tensor_tensor(yy[:, :, n * N:(n + 1) * N], bank(2 * pair, 2).rearrange("p (m n) -> p m n", m=MT),
                                  w[:, n * N:(n + 1) * N].rearrange("p (o n) -> p o n", o=1).broadcast_to([P, MT, N]),
                                  ALU.mult).then_inc(S("y_scaled"), 1)

            for n in range(OUT_BLOCKS):
                for j in range(8):
                    if n == 0:
                        merge(j, OUT_BLOCKS - 1)
                    if n > 0 and j == 5:
                        scale_y(n - 1, y, g1w, 0)
                    split(S_OUT + 8 * n, j)
            for j in range(4):
                split(S_FFN, j)

            def mean_squares(r):
                dve.wait_ge(S("y_square"), 2 * OUT_BLOCKS * r)
                dve.tensor_reduce(ssq[:, 0:MT], ssy[:, :, :], AX_X, ALU.add).then_inc(S("ssy_ready"), 1)
                dve.wait_ge(S("ssy_ready"), 2 * r - 1)
                dve.tensor_scalar(ssq[:, 0:MT], ssq[:, 0:MT], 1.0 / D, EPS, ALU.mult, ALU.add).then_inc(S("ssy_ready"), 1)

            mean_squares(1)
            scale_y(OUT_BLOCKS - 1, y, g1w, 0)
            dve.wait_ge(S("rstd_ready"), 2)
            dve.wait_ge(S("y_scaled"), OUT_BLOCKS)
            for m in range(MT):
                dve.scalar_tensor_tensor(out=hs[:, m, :], in0=y[:, m, :], scalar=rstd[:, m:m + 1], in1=hs[:, m, :],
                                         op0=ALU.mult, op1=ALU.add).then_inc(S("hs_ready"), 1)
            dve.wait_ge(S("partitions_added"), 3)
            dve.tensor_tensor(mod2[:, :, :], bank(6)[:, 0:2 * KT].rearrange("p (a k) -> p a k", a=2),
                              cols2[:, KT:3 * KT].rearrange("p (a k) -> p a k", a=2), ALU.add).then_inc(S("mod2_part"), 1)
            dve.wait_ge(S("mod2_part"), 3)
            dve.scalar_tensor_tensor(out=mod2[:, 1, :], in0=mod2[:, 1, :], scalar=1.0, in1=cols[:, 3 * KT:4 * KT],
                                     op0=ALU.add, op1=ALU.mult).then_inc(S("mod2_part"), 1)
            dve.wait_ge(S("square"), 4 + MT)
            dve.tensor_scalar(ssq[:, 2:4], ssq[:, 2:4], 1.0 / D, EPS, ALU.mult, ALU.add).then_inc(S("ssh_ready"), 1)
            dve.wait_ge(S("rstd_ready"), 3)
            for m in range(MT):
                dve.tensor_scalar(diag[:, m, :], ident[:, :], rstd[:, 2 + m:3 + m], None, ALU.mult).then_inc(S("diag_ready"), 1)
            gate_weight(1, bank(7), 4)

            def hidden(j, n):
                if j == 4:
                    dve.wait_ge(w_used, n * 16 + (S_FFN + 16))
                    dve.wait_ge(S("silu_ready"), n + 1)
                    dve.tensor_tensor(hid_n[:, :, :], bank(0, 2).rearrange("p (m n) -> p m n", m=MT), sg[:, :, :], ALU.mult)\
                        .then_inc(S("hid_n_ready"), 1)
                if j == 6:
                    hh = bass.ds(n * 4, 4)
                    dve.wait_ge(S("turned_hi"), n + (OUT_BLOCKS + 1))
                    dve.tensor_tensor(hid_lo[:, hh, :], bank(4, 2).rearrange("p (q n) -> p q n", q=4),
                                      hid_hi[:, hh, :].bitcast(F32), ALU.subtract).then_inc(S("turned_lo"), 1)

            for j in range(16):
                if j < 8:
                    dve.wait_ge(S("h2_hi_ready"), j + 1)
                    dve.tensor_tensor(h_lo[:, 2 * j:2 * j + 2, :], h2f[:, j % 2, :, :],
                                      h_hi[:, 2 * j:2 * j + 2, :].bitcast(F32), ALU.subtract).then_inc(S("h2_lo_ready"), 1)
                if j >= 4:
                    split(S_FFN, j)
            with dve.Fori(0, FF_BLOCKS - 1) as i:
                for j in range(16):
                    hidden(j, i)
                    split(i * 16 + (S_FFN + 16), j)
            for n in range(OUT_BLOCKS):
                for j in range(DOWN_SLOTS):
                    if n == 0:
                        hidden(j, FF_BLOCKS - 1)
                    if n > 0 and j == 5:
                        scale_y(n - 1, y2, g2w, OUT_BLOCKS)
                    split(S_DOWN + n * DOWN_SLOTS, j)
            mean_squares(2)
            scale_y(OUT_BLOCKS - 1, y2, g2w, OUT_BLOCKS)
            dve.wait_ge(S("rstd_ready"), 4)
            dve.wait_ge(S("y_scaled"), 2 * OUT_BLOCKS)
            for m in range(MT):
                for n in range(OUT_BLOCKS):
                    t = y2[:, m, n * N:(n + 1) * N]
                    dve.scalar_tensor_tensor(out=t, in0=t, scalar=rstd[:, m:m + 1], in1=hs2[:, m, n * N:(n + 1) * N],
                                             op0=ALU.mult, op1=ALU.add).then_inc(S("final_ready"), 1)

        @block.tensor
        def _(pe):
            def products(s, j, k, last_k, tiles, first_bank):
                if isinstance(s, int):
                    s, j = 0, s + j
                q = j % SPLIT
                pe.wait_ge(w_low, s + (j + 1))
                for e in range(2):
                    for n, (hi, lo, m) in enumerate(tiles):
                        o = bank(first_bank + n)
                        kk, c = k + e, slice(m * P, (m + 1) * P)
                        pe.matmul(o, hi[:, kk, c], w_hi[:, q, e, :], start=kk == 0, stop=False)
                        pe.matmul(o, hi[:, kk, c], w_lo[:, q, e, :], start=False, stop=False)
                        last = pe.matmul(o, lo[:, kk, c], w_hi[:, q, e, :], start=False, stop=kk == last_k)
                last.then_inc(w_used, 1)

            LAT = [(h_hi, h_lo, 0), (h_hi, h_lo, 1)]
            CTX = LAT + [(hc_hi, hc_lo, 0), (hc_hi, hc_lo, 1)]

            pe.wait_ge(S("rows_landed"), 16 * 8)
            pe.transpose(bank(7)[:, 0:112], rows[0:112, :], ident[0:112, 0:112]).then_inc(S("cols_turned"), 1)
            pe.wait_ge(S("rows2_landed"), 16 * 4)
            pe.transpose(bank(6)[:, 0:96], rows2[:, :], ident[0:96, 0:96]).then_inc(S("cols_turned"), 1)
            pe.wait_ge(S("c4_ready"), 1)

            def take_mod_columns(n):
                pe.wait_ge(S("mod_row_ready"), n + 1)
                if n == 0:
                    pe.wait_ge(S("cols_ready"), 4)
                if n % 2 == 0 and n > 0:
                    pe.wait_ge(S("mod_ready"), n)
                for r in range(4):
                    k = (n % 2) * KT + (n // 2) * 4 + r
                    last = pe.matmul(bank(6)[:, 2 * k:2 * k + 2], mod_row[:, n, r * P:(r + 1) * P], take[:, :],
                                     start=True, stop=True)
                last.then_inc(S("mod_cols_done"), 1)

            for s, (kind, n, j) in enumerate(opening):
                if kind == "mod":
                    if n >= 2 and j == 0:
                        pe.wait_ge(S("mod_row_ready"), n - 1)
                    pe.wait_ge(w_low, s + 1)
                    for e in range(2):
                        k = 2 * j + e
                        for w in (w_hi, w_lo):
                            last = pe.matmul(bank(4 + n % 2)[0:4, :], c4[:, :, k], w[:, s % SPLIT, e, :],
                                             start=k == 0 and w is w_hi, stop=k == KT - 1 and w is w_lo)
                    last.then_inc(w_used, 1)
                else:
                    pe.wait_ge(S("h1_lo"), 2 * n + j + 1)
                    if n == 0 and j == 0:
                        pe.wait_ge(S("xr_ready_odd"), KT // 2)
                        pe.wait_ge(S("xr_ready"), KT // 2)
                    products(s, 0, 4 * n + 2 * j, KT - 1, CTX, 0)
                if s + 5 in XR_AT:
                    if s + 5 == XR_AT[0]:
                        pe.wait_ge(S("diag_ready"), 4)
                    for k in (2 * XR_AT.index(s + 5), 2 * XR_AT.index(s + 5) + 1):
                        if k >= 4:
                            pe.wait_ge(S("xr_ready_odd" if k % 2 else "xr_ready"), (k - 4) // 2 + 1)
                        for m in range(4):
                            last = pe.matmul(bank(k % 4)[:, m * P:(m + 1) * P], xn[:, m, k * P:(k + 1) * P],
                                             diag0[:, m, :], start=True, stop=True)
                        last.then_inc(S("x_turned"), 1)
                if s - 2 in mod_end and s < mod_end[-1]:
                    take_mod_columns(mod_end.index(s - 2))
                if s == mod_end[-1]:
                    take_mod_columns(MOD_BLOCKS - 1)

            def ctx_block(s, b, group):
                if not isinstance(b, int) or b >= 2:
                    pe.wait_ge(staged[3], b - 1)
                for j in range(8):
                    products(s, j, 2 * j, KT - 1, CTX, 4 * group)

            pe.wait_ge(S("mod_ready"), 2 * QUARTERS)
            ctx_block(S_CTX + 8, 1, 1)
            with pe.Fori(0, 2) as i:
                for u in range(2):
                    ctx_block(i * 16 + (S_CTX + 16 + 8 * u), i * 2 + (2 + u), u)
            ctx_block(S_CTX + 48, 6, 0)
            pe.wait_ge(staged[3], 6)
            pe.wait_ge(S("ga_lo_ready"), 1)
            for n, (hi, lo) in enumerate(((h_hi, h_lo), (hc_hi, hc_lo))):
                o = bank(4)[0:4 * LOW, n * L:(n + 1) * L]
                for k in range(KT):
                    w = ga_hl[:, k, :, :].rearrange("p a c -> p (a c)")
                    pe.matmul(o, w, hi[:, k, :], start=k == 0, stop=False)
                    last = pe.matmul(o, w, lo[:, k, :], start=False, stop=k == KT - 1)
            last.then_inc(S("ga_done"), 1)

            def at_pre(p):
                if p in (4, 10):
                    d = (p - 4) // 6
                    pe.wait_ge(S("al_ready"), 1)
                    pe.wait_ge(S("a_up_landed"), 16 * 5)
                    if d == 1:
                        pe.wait_ge(S("la_ready"), 1)
                    for m in range(4):
                        last = pe.matmul(bank(4 + m), al_t[:, m * P:(m + 1) * P], a_up[:, d, :], start=True, stop=True)
                    last.then_inc(S("z_done"), 1)
                if p in (16, 17):
                    d = p - 16
                    pe.wait_ge(S("la_ready"), 2)
                    if d == 1:
                        pe.wait_ge(S("cum_ready"), 1)
                    for h in range(GH):
                        for m in range(MT):
                            last = pe.matmul(bank(4 + h)[:, 0:L + 1], la[:, d, m, h * GDK:(h + 1) * GDK],
                                             before[:, m, :], start=m == 0, stop=m == MT - 1)
                    last.then_inc(S("sums_done"), 1)
                if p in (18, 19):
                    d = p - 18
                    pe.wait_ge(S("cum_ready"), 2)
                    for q in range(MT):
                        for m in range(MT):
                            t = (after if d == 0 else before)[:, m, q * P:(q + 1) * P]
                            last = pe.matmul(bank(4 + 2 * d + q), t, la[:, d, 2 + m, :], start=m == 0, stop=m == MT - 1)
                    last.then_inc(S("ctx_sums_done"), 1)
                if p == 37:
                    pe.wait_ge(S("wm_used"), 4 * KT)
                    pe.wait_ge(S("kw_exp"), 2)
                    add_partitions(acc, 0, bank(4), 0)
                if p == 40:
                    turn_gate_weight(0, bank(5))

            def add_partitions(sums, g, dst, first):
                for k in range(KT):
                    last = pe.matmul(dst[:, first + k:first + k + 1], sums[:, g, k * P:(k + 1) * P], ones[:, :],
                                     start=True, stop=True)
                last.then_inc(S("partitions_added"), 1)

            def turn_gate_weight(d, dst):
                pe.wait_ge(S("mod2_part"), 2 + 4 * d)
                pe.transpose(dst[0:KT, 0:P], gw_cols[:, d, :], ident[:, :]).then_inc(S("gw_turned"), 1)

            def wait_pair(i, t):
                if isinstance(i, int) and i == 0 and t < 2:
                    pe.wait_ge(staged[3], CTX_BLOCKS)
                else:
                    pe.wait_ge(staged[2 * (t % 2) + 1], i + (CTX_BLOCKS + t // 2))

            def lat_block(s, i, t, at):
                wait_pair(i, t)
                for j in range(8):
                    products(s, j, 2 * j, KT - 1, LAT, 2 * (t % 2))
                    at(j)

            pe.wait_ge(S("ones_ready"), 1)
            pe.wait_ge(S("tables_landed"), 16 * 3)

            def at_head(i, p):
                if p == 0:
                    pe.wait_ge(S("g_qk_landed"), i * 32 + 32)
                    for a, t in enumerate((g_q, g_k)):
                        for m in range(MT):
                            last = pe.transpose(bank(6)[:, a * L + m * P:a * L + (m + 1) * P], t[:, m, :], ident[:, :])
                    last.then_inc(S("g_qk_turned"), 1)
                if p == 2:
                    pe.wait_ge(S("g_qkt_ready"), i * 2 + 2)
                    pe.wait_ge(S("gla_head_done"), i + 1)
                    for m in range(MT):
                        last = pe.matmul(bank(7)[:, m * P:(m + 1) * P], g_qkt[:, 1, m * P:(m + 1) * P],
                                         g_qkt[:, 0, m * P:(m + 1) * P], start=True, stop=True)
                    last.then_inc(S("g_diag_done"), 1)
                    pe.wait_ge(S("g_v_landed"), i * 64 + 64)
                    for d in range(2):
                        for m in range(MT):
                            last = pe.matmul(bank(6)[:, d * GDV:(d + 1) * GDV], g_kw[:, d, m, :], g_v[:, m, :],
                                             start=m == 0, stop=m == MT - 1)
                    last.then_inc(S("g_state_done"), 1)
                if p == 3:
                    pe.wait_ge(S("r_kc_landed"), i * 16 + 16)
                    for f in range(2):
                        for m in range(MT):
                            last = pe.transpose(bank(4)[:, f * L + m * P:f * L + (m + 1) * P],
                                                r_kc[:, m, f * P:(f + 1) * P], ident[:, :])
                    last.then_inc(S("r_kc_turned"), 1)
                if p in (4, 8):
                    r = (p - 4) // 4
                    pe.wait_ge(S("g_qk_ready"), i * 2 + (r + 1))
                    if r == 0:
                        pe.wait_ge(S("g_s_ready"), i + 1)
                        pe.wait_ge(S("g_diag_ready"), i + 1)
                    else:
                        pe.wait_ge(S("g_picked"), i * 7 + 4)
                    for e in range(4):
                        for m in range(MT):
                            key = m
                            qry = m if 4 * r + e < 7 else 1 - m
                            last = pe.matmul(bank(6, 2)[:, e * L + m * P:e * L + (m + 1) * P],
                                             g_arg[:, 1, e, key * P:(key + 1) * P], g_arg[:, 0, e, qry * P:(qry + 1) * P],
                                             start=True, stop=True)
                    last.then_inc(S("g_levels_done"), 1)
                if p == 6:
                    pe.wait_ge(S("rope_ready"), i * 4 + 4)
                    pe.wait_ge(S("ret_head_done"), i + 1)
                    pe.wait_ge(S("r_kct_ready"), i + 1)
                    for b, t in ((5, r_q), (4, r_k)):
                        for f in range(2):
                            for m in range(MT):
                                last = pe.transpose(bank(b)[:, f * L + m * P:f * L + (m + 1) * P],
                                                    t[:, m, f * P:(f + 1) * P], ident[:, :])
                    last.then_inc(S("r_qk_turned"), 1)
                if p == 10:
                    pe.wait_ge(S("g_picked"), i * 7 + 7)
                    pe.wait_ge(S("g_cross_ready"), i + 1)
                    pe.wait_ge(S("g_st_ready"), i + 1)
                    for m in range(MT):
                        o, c = bank(6)[:, m * GDV:(m + 1) * GDV], slice(m * P, (m + 1) * P)
                        pe.matmul(o, g_a[:, m, :], g_v[:, 2 + m, :], start=True, stop=False)
                        pe.matmul(o, g_a[:, 3 - m, :], g_v[:, 3 - m, :], start=False, stop=False)
                        pe.matmul(o, g_st[:, 0, c], g_s[:, 0, :], start=False, stop=False)
                        last = pe.matmul(o, g_st[:, 1, c], g_s[:, 1, :], start=False, stop=True)
                    last.then_inc(S("g_o_done"), 1)
                if p == 7:
                    pe.wait_ge(S("r_qkt_ready"), i * 2 + 2)
                    for a in range(4):
                        for f in range(2):
                            last = pe.matmul(bank(4, 2)[:, a * L:(a + 1) * L],
                                             r_kt[:, 2 * (a // 2) + f, (a % 2) * P:(a % 2 + 1) * P], r_qt[:, f, :],
                                             start=f == 0, stop=f == 1)
                    last.then_inc(S("r_scores_done"), 1)
                if p == 14:
                    pe.wait_ge(S("g_on_ready"), i + 1)
                    for f in range(2):
                        for m in range(MT):
                            last = pe.transpose(bank(7)[:, f * L + m * P:f * L + (m + 1) * P],
                                                g_g[:, m, f * P:(f + 1) * P], ident[:, :])
                    last.then_inc(S("g_on_turned"), 1)
                if p == 9:
                    pe.wait_ge(S("r_a_ready"), i + 1)
                    pe.wait_ge(S("r_v_landed"), i * 32 + 32)
                    for m in range(MT):
                        for a in range(4):
                            last = pe.matmul(bank(4)[:, m * RDK:(m + 1) * RDK], r_a[:, a, m * P:(m + 1) * P],
                                             r_v[:, a, :], start=a == 0, stop=a == 3)
                    last.then_inc(S("r_o_done"), 1)
                if p == 13:
                    pe.wait_ge(S("r_on_ready"), i + 1)
                    for f in range(2):
                        for m in range(MT):
                            last = pe.transpose(bank(5)[:, f * L + m * P:f * L + (m + 1) * P],
                                                r_g[:, m, f * P:(f + 1) * P], ident[:, :])
                    last.then_inc(S("r_on_turned"), 1)

            def head_pass(s, i):
                for u in range(2):
                    for j in range(8):
                        p = 8 * u + j + 4
                        if j == 0:
                            wait_pair(i, 7 + u)
                        products(s, 8 * u + j, 2 * j, KT - 1, LAT, 2 * ((7 + u) % 2))
                        if p < 16:
                            at_head(i, p)
                        elif not isinstance(i, int):
                            at_head(i + 1, p - 16)

            for t in range(7):
                if t == 6:
                    pe.wait_ge(S("gw_rows_ready"), 1)
                lat_block(S_LAT + 8 * t, 0, t, lambda j: at_head(0, j - 4) if t == 6 and j >= 4 else at_pre(8 * t + j + 4))
            with pe.Fori(0, RH - 1) as i:
                head_pass(i * 16 + (S_LAT + 56), i)
            head_pass(S_LAT + 16 * (RH - 1) + 56, RH - 1)

            def turn_columns(src, ready, n):
                pe.wait_ge(S(ready), n + 1)
                for q in range(4):
                    for m in range(MT):
                        last = pe.transpose(bank(4, 2)[:, q * L + m * P:q * L + (m + 1) * P],
                                            src[:, m, q * P:(q + 1) * P], ident[:, :])
                last.then_inc(S("turned"), 1)

            def up_block(s, n, prev):
                for g in range(2):
                    pe.wait_ge(S("o_lo_ready"), g + 1)
                    if prev is None:
                        pe.wait_ge(staged[3 - 2 * g], 14 + g)
                    else:
                        pe.wait_ge(S(f"gate_used{g}"), n)
                    for j in range(4):
                        tiles = [(o_hi[:, g], o_lo[:, g], 0), (o_hi[:, g], o_lo[:, g], 1)]
                        products(s, 4 * g + j, 2 * j, 7, tiles, 2 - 2 * g)
                        if prev is not None and g == 0 and j == 2:
                            turn_columns(mg, "mg_ready", prev)
            up_block(S_UP, 0, None)
            with pe.Fori(0, OUT_BLOCKS - 1) as i:
                up_block(i * 8 + (S_UP + 8), i + 1, i)

            for n in range(OUT_BLOCKS):
                if n < 2:
                    pe.wait_ge(S(f"gate_used{n}"), OUT_BLOCKS)
                else:
                    pe.wait_ge(S("y_scaled"), n - 1)
                for j in range(8):
                    if n == 0 and j in (0, 6):
                        pe.wait_ge(S("turned_lo"), 3 if j == 0 else 4)
                    products(S_OUT + 8 * n, j, 2 * j, KT - 1, LAT, 2 * (1 - n % 2))
                    if n == 0 and j == 2:
                        turn_columns(mg, "mg_ready", OUT_BLOCKS - 1)

            def turn_h2(j):
                if j == 0:
                    pe.wait_ge(S("diag_ready"), 4 + MT)
                if j == 3:
                    pe.wait_ge(S("mod2_part"), 5)
                if j >= 4:
                    pe.wait_ge(S("h2_hi_ready"), j - 3)
                for e in range(2):
                    for m in range(MT):
                        last = pe.matmul(bank(4 + j % 4)[:, e * L + m * P:e * L + (m + 1) * P],
                                         hs[:, m, (2 * j + e) * P:(2 * j + e + 1) * P], diag[:, m, :], start=True, stop=True)
                last.then_inc(S("h2_turned"), 1)

            pe.wait_ge(S("acc_landed"), 16)
            add_partitions(acc2, 0, bank(6), 0)
            add_partitions(acc2, 1, bank(6), KT)
            add_partitions(acc2, 2, bank(7), 0)
            for j in range(3):
                turn_h2(j)

            def ffn_block(s, n, prev):
                for g in range(2):
                    if prev is not None:
                        pe.wait_ge(S("silu_ready" if g == 0 else "hid_n_ready"), n)
                    else:
                        pe.wait_ge(S("y_scaled"), OUT_BLOCKS)
                    for j in range(8):
                        if prev is None and g == 0:
                            pe.wait_ge(S("h2_lo_ready"), j + 1)
                        products(s, 8 * g + j, 2 * j, KT - 1, LAT, 2 - 2 * g)
                        if prev is None and g == 0 and j < 5:
                            turn_h2(j + 3)
                        if prev is None and g == 1 and j == 2:
                            pe.wait_ge(S("h2_hi_ready"), 8)
                            turn_gate_weight(1, bank(6))
                        if prev is not None and g == 0 and j == 2:
                            turn_columns(hid_n, "hid_n_ready", prev)
            ffn_block(S_FFN, 0, None)
            with pe.Fori(0, FF_BLOCKS - 1) as i:
                ffn_block(i * 16 + (S_FFN + 16), i + 1, i)

            for n in range(OUT_BLOCKS):
                if n == 0:
                    pe.wait_ge(S("silu_ready"), FF_BLOCKS)
                elif n == 1:
                    pe.wait_ge(S("hid_n_ready"), FF_BLOCKS)
                else:
                    pe.wait_ge(S("y_scaled"), OUT_BLOCKS + n - 1)
                HID = [(hid_hi, hid_lo, 0), (hid_hi, hid_lo, 1)]
                for j in range(DOWN_SLOTS):
                    if n == 0 and j in (0, 20):
                        pe.wait_ge(S("turned_lo"), OUT_BLOCKS + FF_BLOCKS - (j == 0))
                    products(S_DOWN + n * DOWN_SLOTS, j, 2 * j, D_FF // P - 1, HID, 2 * (1 - n % 2))
                    if n == 0 and j == 2:
                        turn_columns(hid_n, "hid_n_ready", FF_BLOCKS - 1)


STACKED = ["w_mod", "b_mod", "norm_mix_pre", "norm_mix_post", "norm_ffn_pre", "norm_ffn_post", "w_in", "ret_decay",
        "gla_a_up", "gla_a_bias", "ret_gn", "gla_gn", "w_up_ret", "w_up_gla", "w_out", "ffn_w_gate", "ffn_w_up",
        "ffn_w_down"]


def kernel(**inputs):
    import concourse.bacc as bacc
    from concourse.bass_utils import run_bass_kernel_spmd as run

    nc = bacc.Bacc("TRN2", target_bir_lowering=False, num_devices=1)
    arrays = {"x": np.asarray(inputs["x"])[0], "c": np.asarray(inputs["c"])[0],
              "ctx_in": np.asarray(inputs["ctx"])[0], "c_ctx": np.asarray(inputs["c_ctx"])}
    arrays.update({n: np.asarray(inputs[n])[0] for n in STACKED})
    arrays.update(constants())
    arrays = {n: np.ascontiguousarray(a) for n, a in arrays.items()}
    args = {n: nc.dram_tensor(f"in_{n}", a.shape, mybir.dt.from_np(a.dtype), kind="ExternalInput").ap()
            for n, a in arrays.items()}
    out = nc.dram_tensor("result", (L, D), F32, kind="ExternalOutput").ap()
    build(nc, **args, out=out)
    r = run(nc, [{f"in_{n}": a for n, a in arrays.items()}], core_ids=[0])
    return r.results[0]["result"][None]
```
